# Optimizing a Trainium2 kernel written in Bass

```python
import math
import jax, jax.numpy as jnp
from jax import lax
import numpy as np

D_MODEL = 1024
BATCH = 1
SEQ = 512
DEPTH = 2
DEC_BATCH = 1
DEC_SEQ = 512
PAST_LEN = 128

DIFF_HEADS = 4
DIFF_DH = 64
DIFF_DV = 2 * DIFF_DH
DIFF_WIDTH = DIFF_HEADS * DIFF_DV
MLA_HEADS = 4
MLA_NOPE = 128
MLA_ROPE = 64
MLA_V = 128
Q_LORA = 256
KV_LORA = 128
MLA_WIDTH = MLA_HEADS * MLA_V
MIX_WIDTH = DIFF_WIDTH + MLA_WIDTH
IN_COLS = 3 * DIFF_WIDTH + Q_LORA + KV_LORA + MLA_ROPE
D_FF = ((8 * D_MODEL + 3 * 256 - 1) // (3 * 256)) * 256
ROPE_THETA = 10000.0
Q_BLOCK = 128
EPS = 1e-6

kernel_name = "hybrid_diffattn_mla_encoder"

def _rms(x, g):
    xf = x.astype(jnp.float32)
    y = xf * lax.rsqrt(jnp.mean(xf * xf, axis=-1, keepdims=True) + EPS)
    return (y * g.astype(jnp.float32)).astype(x.dtype)

def _rope(x, pos):
    d = x.shape[-1]
    half = d // 2
    inv = 1.0 / (ROPE_THETA ** (jnp.arange(half, dtype=jnp.float32) * 2.0 / d))
    ang = pos.astype(jnp.float32)[:, None] * inv[None, :]
    cos = jnp.cos(ang)[None, :, None, :]
    sin = jnp.sin(ang)[None, :, None, :]
    xf = x.astype(jnp.float32)
    x1, x2 = xf[..., :half], xf[..., half:]
    out = jnp.concatenate([x1 * cos - x2 * sin, x2 * cos + x1 * sin], axis=-1)
    return out.astype(x.dtype)

def _to_blocks(t):
    b, s = t.shape[:2]
    return t.reshape((b, s // Q_BLOCK, Q_BLOCK) + t.shape[2:]).swapaxes(0, 1)

def _from_blocks(t):
    nb, b, qb = t.shape[:3]
    return t.swapaxes(0, 1).reshape((b, nb * qb) + t.shape[3:])

def _diff_attention(q, k, v, lam, subln_g, lam_init):
    b, s = q.shape[:2]
    q = q.reshape(b, s, DIFF_HEADS, 2, DIFF_DH)
    k = k.reshape(b, s, DIFF_HEADS, 2, DIFF_DH)
    scale = DIFF_DH ** -0.5

    def blk(qb):
        sc = jnp.einsum('bqhcd,bkhcd->bhcqk', qb, k).astype(jnp.float32) * scale
        p = jax.nn.softmax(sc, axis=-1)
        a = p[:, :, 0] - lam * p[:, :, 1]
        return jnp.einsum('bhqk,bkhe->bqhe', a.astype(v.dtype), v)

    o = _from_blocks(lax.map(blk, _to_blocks(q)))
    o = _rms(o, subln_g) * (1.0 - lam_init)
    return o.reshape(b, s, DIFF_WIDTH)

def _mla_attention(q_nope, q_pe, k_nope, k_pe, v):
    b, s = q_nope.shape[:2]
    scale = (MLA_NOPE + MLA_ROPE) ** -0.5

    def blk(qs):
        qn, qp = qs
        sc = (jnp.einsum('bqhd,bkhd->bhqk', qn, k_nope)
              + jnp.einsum('bqhr,bkr->bhqk', qp, k_pe)).astype(jnp.float32) * scale
        p = jax.nn.softmax(sc, axis=-1)
        return jnp.einsum('bhqk,bkhd->bqhd', p.astype(v.dtype), v)

    o = _from_blocks(lax.map(blk, (_to_blocks(q_nope), _to_blocks(q_pe))))
    return o.reshape(b, s, MLA_WIDTH)

def _layer(x, pos, l, attn_norm, w_in, lam_q1, lam_k1, lam_q2, lam_k2, diff_subln,
           q_a_norm, w_q_b, kv_a_norm, w_kv_b, w_o, ffn_norm, w_gate, w_up, w_down):
    b, s, _ = x.shape
    h = _rms(x, attn_norm[l])
    z = h @ w_in[l]
    o1 = DIFF_WIDTH
    o2 = o1 + DIFF_WIDTH
    o3 = o2 + DIFF_WIDTH
    o4 = o3 + Q_LORA
    o5 = o4 + KV_LORA
    dq = _rope(z[..., :o1].reshape(b, s, 2 * DIFF_HEADS, DIFF_DH), pos)
    dk = _rope(z[..., o1:o2].reshape(b, s, 2 * DIFF_HEADS, DIFF_DH), pos)
    dv = z[..., o2:o3].reshape(b, s, DIFF_HEADS, DIFF_DV)
    c_q = z[..., o3:o4]
    c_kv = z[..., o4:o5]
    k_pe = z[..., o5:]

    lam_init = 0.8 - 0.6 * math.exp(-0.3 * l)
    lam = (jnp.exp(jnp.sum(lam_q1[l].astype(jnp.float32) * lam_k1[l].astype(jnp.float32)))
           - jnp.exp(jnp.sum(lam_q2[l].astype(jnp.float32) * lam_k2[l].astype(jnp.float32)))
           + lam_init)
    y_diff = _diff_attention(dq, dk, dv, lam, diff_subln[l], lam_init)

    qh = (_rms(c_q, q_a_norm[l]) @ w_q_b[l]).reshape(b, s, MLA_HEADS, MLA_NOPE + MLA_ROPE)
    q_nope = qh[..., :MLA_NOPE]
    q_pe = _rope(qh[..., MLA_NOPE:], pos)
    kvh = (_rms(c_kv, kv_a_norm[l]) @ w_kv_b[l]).reshape(b, s, MLA_HEADS, MLA_NOPE + MLA_V)
    k_nope = kvh[..., :MLA_NOPE]
    v = kvh[..., MLA_NOPE:]
    k_pe = _rope(k_pe[:, :, None, :], pos)[:, :, 0, :]
    y_mla = _mla_attention(q_nope, q_pe, k_nope, k_pe, v)

    x = x + jnp.concatenate([y_diff, y_mla], axis=-1) @ w_o[l]

    h = _rms(x, ffn_norm[l])
    x = x + (jax.nn.silu(h @ w_gate[l]) * (h @ w_up[l])) @ w_down[l]
    return x

def _trunk(x, attn_norm, w_in, lam_q1, lam_k1, lam_q2, lam_k2, diff_subln,
           q_a_norm, w_q_b, kv_a_norm, w_kv_b, w_o, ffn_norm, w_gate, w_up, w_down, final_norm):
    pos = jnp.arange(x.shape[1], dtype=jnp.int32)
    for l in range(DEPTH):
        x = _layer(x, pos, l, attn_norm, w_in, lam_q1, lam_k1, lam_q2, lam_k2, diff_subln,
                   q_a_norm, w_q_b, kv_a_norm, w_kv_b, w_o, ffn_norm, w_gate, w_up, w_down)
    return _rms(x, final_norm)

def setup_inputs(seed: int = 0) -> dict:
    key = jax.random.key(seed)
    ks = jax.random.split(key, 20)
    f32 = jnp.float32

    def w(k, shape, fan_in):
        return jax.random.normal(k, shape, f32) * (fan_in ** -0.5)

    def gain(k, shape):
        return 1.0 + 0.05 * jax.random.normal(k, shape, f32)

    return {
        "x_prompt": jax.random.normal(ks[0], (BATCH, SEQ, D_MODEL), f32),
        "x_sample": jax.random.normal(ks[1], (DEC_BATCH, DEC_SEQ, D_MODEL), f32),
        "attn_norm": gain(ks[2], (DEPTH, D_MODEL)),
        "w_in": w(ks[3], (DEPTH, D_MODEL, IN_COLS), D_MODEL),
        "lam_q1": 0.1 * jax.random.normal(ks[4], (DEPTH, DIFF_DH), f32),
        "lam_k1": 0.1 * jax.random.normal(ks[5], (DEPTH, DIFF_DH), f32),
        "lam_q2": 0.1 * jax.random.normal(ks[6], (DEPTH, DIFF_DH), f32),
        "lam_k2": 0.1 * jax.random.normal(ks[7], (DEPTH, DIFF_DH), f32),
        "diff_subln": gain(ks[8], (DEPTH, DIFF_DV)),
        "q_a_norm": gain(ks[9], (DEPTH, Q_LORA)),
        "w_q_b": w(ks[10], (DEPTH, Q_LORA, MLA_HEADS * (MLA_NOPE + MLA_ROPE)), Q_LORA),
        "kv_a_norm": gain(ks[11], (DEPTH, KV_LORA)),
        "w_kv_b": w(ks[12], (DEPTH, KV_LORA, MLA_HEADS * (MLA_NOPE + MLA_V)), KV_LORA),
        "w_o": w(ks[13], (DEPTH, MIX_WIDTH, D_MODEL), MIX_WIDTH),
        "ffn_norm": gain(ks[14], (DEPTH, D_MODEL)),
        "w_gate": w(ks[15], (DEPTH, D_MODEL, D_FF), D_MODEL),
        "w_up": w(ks[16], (DEPTH, D_MODEL, D_FF), D_MODEL),
        "w_down": w(ks[17], (DEPTH, D_FF, D_MODEL), D_FF),
        "final_norm": gain(ks[18], (D_MODEL,)),
    }

def reference(x_prompt, x_sample, attn_norm, w_in, lam_q1, lam_k1, lam_q2, lam_k2, diff_subln,
              q_a_norm, w_q_b, kv_a_norm, w_kv_b, w_o, ffn_norm, w_gate, w_up, w_down, final_norm):
    y_prompt = _trunk(x_prompt, attn_norm, w_in, lam_q1, lam_k1, lam_q2, lam_k2, diff_subln,
                      q_a_norm, w_q_b, kv_a_norm, w_kv_b, w_o, ffn_norm, w_gate, w_up, w_down, final_norm)
    y_sample = _trunk(x_sample, attn_norm, w_in, lam_q1, lam_k1, lam_q2, lam_k2, diff_subln,
                      q_a_norm, w_q_b, kv_a_norm, w_kv_b, w_o, ffn_norm, w_gate, w_up, w_down, final_norm)
    return (y_prompt, y_sample)


_drawn_inputs = setup_inputs


def setup_inputs(seed=0):
    import zlib

    import numpy as np

    out = dict(_drawn_inputs(seed))
    spreads = {}
    factors = {'q_a_norm': 8.0, 'kv_a_norm': 5.657}
    for name, (base, spread) in spreads.items():
        noise = np.random.default_rng([zlib.crc32(name.encode()), seed]).standard_normal(out[name].shape)
        drawn = base * np.exp(spread * noise) if base else spread * noise
        out[name] = __import__('jax').numpy.asarray(drawn.astype(out[name].dtype))
    for name, factor in factors.items():
        out[name] = (out[name] * factor).astype(out[name].dtype)
    return out
```

```python
from contextlib import ExitStack
import math

import numpy as np

import concourse.bass as bass
from concourse import mybir
from concourse.alu_op_type import AluOpType as ALU

ACT = mybir.ActivationFunctionType
F32 = mybir.dt.float32
F32R = mybir.dt.float32r
I32 = mybir.dt.int32
AX_X = mybir.AxisListType.X

P = 128
D = 1024
KT = D // P
T = 512
NT = T // P
L = 2
B = 2
H = 4
DH = 64
ROPE = 64
NOPE = 128
QL = 256
KVL = 128
FF = 2816
FT = FF // P
FC = FT // 2
CH = 1024
EPS = 1e-6
DIFF_SCALE = DH ** -0.5
MLA_SCALE = (NOPE + ROPE) ** -0.5
LAM_INIT = [0.8 - 0.6 * math.exp(-0.3 * l) for l in range(L)]
SEED = 64

CHUNKS = ([f"dv{j}" for j in range(4)] + [f"{x}{h}" for h in range(H) for x in "qk"]
          + ["kpe", "ckv", "cq0", "cq1", "pe", "qn", "kvb"]
          + [f"oa{j}" for j in range(4)] + [f"ob{j}" for j in range(4)])
NCH = len(CHUNKS)
FCH = 6
RAW = 3
WS_ATT = 3
WS_FFN = 6
assert NCH % RAW == 0 and NCH % WS_ATT == 0 and FCH % RAW == 0 and FCH % WS_FFN == 0
CHUNKS_LAYER = B * NCH + FC * FCH

UNITS = 2 * H * NT


def attention_order():
    o = [("V",), ("P", "q0"), ("P", "k0")]
    fill = {}
    for h in range(3):
        fill[4 * h] = [("Pa", f"q{h + 1}")]
        fill[4 * h + 1] = [("Pb", f"q{h + 1}")]
        fill[4 * h + 2] = [("Pa", f"k{h + 1}")]
        fill[4 * h + 3] = [("Pb", f"k{h + 1}")]
    fill[5] = [("RB", "y0")] + fill[5]
    fill[9] = [("RB", "y1")] + fill[9]
    fill[12] = [("P", "kpe")]
    fill[13] = [("RB", "y2"), ("P", "ckv")]
    fill[14] = [("ST", "ckv"), ("P", "cq0")]
    fill[15] = [("RB", "ckv"), ("P", "cq1")]
    fill[17] = [("RB", "y3"), ("P", "kn1"), ("P", "qn1")]
    fill[18] = [("P", "oa0")]
    fill[19] = [("P", "oa1")]
    fill[20] = [("P", "kn2"), ("P", "qn2")]
    fill[24] = [("P", "kn3"), ("P", "qn3")]
    fill[25] = [("P", "oa2")]
    fill[27] = [("P", "oa3")]
    fill[29] = [("P", "oa4")]
    fill[30] = [("P", "oa5")]
    for i in range(UNITS):
        if i == 16:
            o += [("ST", "cq"), ("T", 15), ("A", 7), ("YC", 3), ("RB", "cq"), ("P", "kn0"), ("P", "vm0"), ("P", "vm1"),
                  ("P", "pe0"), ("P", "vm2"), ("P", "vm3"), ("P", "pe1"), ("P", "qn0"), ("YD", 3)]
        o.append(("S", i))
        o += fill.get(i, [])
        if i not in (0, 16):
            u = i - 1
            o.append(("T", u))
            if u % 2:
                o.append(("A", u // 2))
            if u % 4 == 3:
                o += [("YC", u // 4)]
                if u < 16:
                    o += [("YD", u // 4)]
    o += [("P", "oa6"), ("T", 31), ("P", "oa7"), ("A", 15), ("YC", 7)]
    o += [("P", "ob0"), ("NQ",), ("P", "ob1"), ("ST", "n"), ("P", "ob2"), ("P", "ob3"), ("RB", "n"), ("P", "ob4"),
          ("NA",), ("P", "ob5"), ("P", "ob6"), ("P", "ob7")]
    return o


ORDER = attention_order()
STATS = ["y0", "y1", "y2", "ckv", "cq", "y3", "n"]
assert [s[1] for s in ORDER if s[0] == "RB"] == STATS, [s[1] for s in ORDER if s[0] == "RB"]
NSTAT = len(STATS)
TILES = [s[1] for s in ORDER if s[0] in ("P", "Pa")]
TILE = {n: i for i, n in enumerate(TILES)}
NTILE = len(TILES)
assert NTILE == 42 and NTILE % 2 == 0


def numbered(names):
    return {n: i for i, n in enumerate(names)}


DV_MM = 7
ROPED = numbered([t for t in TILES if t[0] in "qk" and t[1].isdigit() or t in ("kpe", "pe0", "pe1")])
ROPE_SPLITS = numbered([(t, c) for t in ROPED for c in range(2 if t[0] in "qp" else 1)])
PLAIN = numbered(["dv0", "dv1", "dv2", "dv3"] + [t for t in TILES if t[:2] in ("kn", "qn", "vm")])
LATENT = numbered([t for t in TILES if t[0] == "c"])
OUTS = numbered([t for t in TILES if t[0] == "o"])
SQUARES = {}
for _s in STATS:
    _n = {"n": KT, "cq": 2}.get(_s, 1)
    _at = sum(len(v) for v in SQUARES.values())
    SQUARES[_s] = list(range(_at, _at + _n))
NSQ = sum(len(v) for v in SQUARES.values())
NSQ_LAYER = B * NSQ + 2 * KT
ADDS = {"cq": [0], "n": list(range(1, 1 + KT))}
NADD = 1 + KT
NADD_LAYER = B * NADD + 2 * KT
NSTAT_LAYER = B * NSTAT + 2
NEV = 2 * 16 + 16
RSQRT_LINKS = 12


def chunk_of(tile):
    if tile in ("pe0", "pe1"):
        return CHUNKS.index("pe")
    if tile[:2] == "qn":
        return CHUNKS.index("qn")
    if tile[:2] in ("kn", "vm"):
        return CHUNKS.index("kvb")
    if tile[0] == "o":
        return CHUNKS.index(tile[:2] + str(int(tile[2]) // 2))
    return CHUNKS.index(tile)


CHUNK_FREE = [0, 1, 2, 6] + [DV_MM + max(TILE[t] for t in TILES if chunk_of(t) == j) for j in range(4, NCH)]
NMM = DV_MM + NTILE
FMM = 8 + 2 * KT
FCHUNK_FREE = [2, 3, 6, 7, FMM - 1, FMM - 1]
PRE_LAM = 4
PRE_DVE = PRE_LAM + 4 * L
FINAL = KT + RSQRT_LINKS + 1 + KT
FINAL_ADD = [FINAL * b + KT for b in range(B)]
FINAL_DG = [FINAL * b + KT + RSQRT_LINKS + 1 for b in range(B)]
FINAL_T = [FINAL_DG[b] + k + 1 for b in range(B) for k in range(KT)]
FINAL_SQ = [FINAL * b + k - 1 if k >= 2 else FINAL_ADD[0] * b for b in range(B) for k in range(KT)]


class Count:

    def __init__(self, sem, half=0, step=0, layer=None, seed=SEED, before=0, unit=1):
        self.sem, self.half, self.step, self.seed, self.before, self.unit = sem, half, step, seed, before, unit
        self.layer = layer if layer is not None else B * half + FC * step

    def half_at(self, l, b, j):
        return l * (self.layer * self.unit) + b * (self.half * self.unit) + (self.seed + (self.before + j + 1) * self.unit)

    def step_at(self, l, c, j):
        at = self.before + B * self.half
        return l * (self.layer * self.unit) + c * (self.step * self.unit) + (self.seed + (at + j + 1) * self.unit)

    def layer_at(self, l, j):
        return l * (self.layer * self.unit) + (self.seed + (j + 1) * self.unit)


def encoder_trunk(nc, xT, watt, wffn, tables, gains, lam, out):
    with ExitStack() as ctx:
        KB = 1024
        cursor = [nc.sbuf_base + (-nc.sbuf_base) % 64]

        def region(size):
            at = cursor[0]
            cursor[0] += size
            return at

        def at(name, shape, offset, dt=F32):
            return nc.alloc_sbuf_tensor_at(name, shape, dt, offset=offset)

        def psum(name):
            return ctx.enter_context(nc.psum_tensor(name, [P, T], F32))

        r_x = region(32 * KB)
        r_h = region(32 * KB)
        r_yv = region(32 * KB)
        r_raw = region(RAW * 4 * KB)
        r_w = region(WS_ATT * 8 * KB)
        r_qk = region(24 * KB)
        r_at = region(16 * KB)
        r_e = region(8 * KB)
        r_ckv = region(4 * KB)
        r_s = region(16 * KB)
        r_c = region(4 * KB + 1024 + 256 * 5 )
        assert cursor[0] <= nc.sbuf_usable_end, (cursor[0], nc.sbuf_usable_end)

        x = at("x", [P, B, KT, T], r_x)
        h0 = [at(f"h0_{s}", [P, KT, T], r_h + i * 16 * KB, F32R) for i, s in enumerate(("hi", "lo"))]
        h1 = [at(f"h1_{s}", [P, KT, T], r_yv + i * 16 * KB, F32R) for i, s in enumerate(("hi", "lo"))]
        ydiff = [at(f"ydiff_{s}", [P, H, T], r_yv + i * 8 * KB, F32R) for i, s in enumerate(("hi", "lo"))]
        v = [at(f"v_{s}", [P, NT, H * P], r_yv + (16 + i * 8) * KB, F32R) for i, s in enumerate(("hi", "lo"))]
        raw = at("raw", [P, RAW, CH], r_raw)
        w = [[at(f"w_{s}{n}", [P, CH], r_w + (n * 8 + i * 4) * KB, F32R) for i, s in enumerate(("hi", "lo"))]
             for n in range(WS_FFN)]
        qd = [[[at(f"qd{n}{c}_{s}", [P, T], r_qk + (n * 12 + c * 4 + i * 2) * KB, F32R)
                for i, s in enumerate(("hi", "lo"))] for c in range(2)] for n in range(2)]
        kd = [[at(f"kd{n}_{s}", [P, T], r_qk + (n * 12 + 8 + i * 2) * KB, F32R)
               for i, s in enumerate(("hi", "lo"))] for n in range(2)]
        cq = [[at(f"cq{n}_{s}", [P, T], r_qk + (n * 4 + i * 2) * KB, F32R)
               for i, s in enumerate(("hi", "lo"))] for n in range(2)]
        kpe = [at(f"kpe_{s}", [P, T], r_qk + (8 + i * 2) * KB, F32R) for i, s in enumerate(("hi", "lo"))]
        ckv = [at(f"ckv_{s}", [P, T], r_ckv + i * 2 * KB, F32R) for i, s in enumerate(("hi", "lo"))]
        ymla = [[at(f"ymla{n}_{s}", [P, T], (r_qk + (12 + n * 4 + i * 2) * KB) if n < 3 else r_ckv + i * 2 * KB, F32R)
                 for i, s in enumerate(("hi", "lo"))] for n in range(H)]
        qpe = [[at(f"qpe{n}_{s}", [P, T], r_h + (n * 4 + i * 2) * KB, F32R)
                for i, s in enumerate(("hi", "lo"))] for n in range(H)]
        qn = [[at(f"qn{n}_{s}", [P, T], r_h + (16 + n * 4 + i * 2) * KB, F32R)
               for i, s in enumerate(("hi", "lo"))] for n in range(2)]
        kn = [[at(f"kn{n}_{s}", [P, T], r_h + (24 + n * 4 + i * 2) * KB, F32R)
               for i, s in enumerate(("hi", "lo"))] for n in range(2)]
        aT = [[at(f"aT{n}_{s}", [P, NT, 2 * P], r_at + (n * 8 + i * 4) * KB, F32R)
               for i, s in enumerate(("hi", "lo"))] for n in range(2)]
        u = [[[at(f"u{t}{b}_{s}", [P, T], r_at + (t * 8 + b * 4 + i * 2) * KB, F32R)
               for i, s in enumerate(("hi", "lo"))] for b in range(B)] for t in range(2)]
        e = [at(f"e{n}", [P, T], r_e + n * 2 * KB) for n in range(4)]
        silu = [at(f"silu{n}", [P, T], r_e + n * 2 * KB) for n in range(2)]
        gated = [at(f"gated{n}", [P, T], r_e + (4 + n * 2) * KB) for n in range(2)]
        sq = [at(f"sq{n}", [P, T], r_s + n * 2 * KB) for n in range(2)]
        acc = at("acc", [P, T], r_s + 4 * KB)
        dg = at("dg", [P, NT, P], r_s + 6 * KB)
        t = [at(f"t{n}", [P, T], r_s + (8 + n * 2) * KB) for n in range(2)]
        r1 = at("r1", [P, T], r_s + 12 * KB)
        r2 = at("r2", [P, T], r_s + 14 * KB)
        cs = at("cs", [P, 2, T], r_c)
        small = [r_c + 4 * KB]

        def little(name, n, dt=F32):
            o = small[0]
            small[0] += -(-n * 4 // 32) * 32
            assert small[0] <= cursor[0], name
            return at(name, [P, n], o, dt)

        ident = little("ident", P)
        masks = little("masks", 4)
        ones = little("ones", P)
        g = little("g", 4 * L * KT + KT)
        gsmall = little("gsmall", L * 4)
        gsub = little("gsub", L)
        lamv = little("lamv", 2 * L)
        mx = little("mx", NEV)
        ls = little("ls", NEV)
        rc = little("rc", 4)
        ms = [little(f"ms{n}", NT) for n in range(3)]
        yi = little("yi", NT, I32)
        yy = little("yy", NT)
        zero = little("zero", 1)
        lamt = e[0]

        bank = [psum(f"bank{n}") for n in range(8)]
        tail = 7

        def sem(name):
            return ctx.enter_context(nc.semaphore(name))

        s_load = sem("constants_loaded")
        s_xload = sem("x_loaded")
        s_raw = [Count(sem(f"raw_loaded{n}"), half=NCH // RAW, step=FCH // RAW, seed=0, unit=16) for n in range(RAW)]
        s_hi = Count(sem("weights_hi"), NCH, FCH)
        s_lo = Count(sem("weights_lo"), NCH, FCH)
        s_mm = Count(sem("projection_done"), NMM, FMM)
        s_plain_hi = Count(sem("plain_hi"), len(PLAIN))
        s_plain_lo = Count(sem("plain_lo"), len(PLAIN))
        s_rope_read = Count(sem("rope_bank_read"), len(ROPED))
        s_roped = Count(sem("roped"), len(ROPED))
        s_rope_hi = Count(sem("rope_hi"), len(ROPE_SPLITS))
        s_rope_lo = Count(sem("rope_lo"), len(ROPE_SPLITS))
        s_latent = Count(sem("latent_copied"), len(LATENT))
        s_xo = Count(sem("output_added"), len(OUTS))
        s_score = Count(sem("scores_done"), NEV)
        s_max = Count(sem("max_done"), NEV)
        s_exp = Count(sem("exp_done"), NEV)
        s_prob = Count(sem("probs_done"), UNITS)
        s_tr = Count(sem("transposed"), UNITS)
        s_at_hi = Count(sem("aT_hi"), UNITS)
        s_at_lo = Count(sem("aT_lo"), UNITS)
        s_av = Count(sem("av_done"), UNITS // 2)
        s_oc = Count(sem("diff_out_copied"), H)
        s_ym_hi = Count(sem("latent_out_hi"), H)
        s_ym_lo = Count(sem("latent_out_lo"), H)
        s_sq = Count(sem("squares"), NSQ, layer=NSQ_LAYER, before=KT)
        s_add = Count(sem("squares_added"), NADD, layer=NADD_LAYER, before=KT)
        s_st = Count(sem("sums_done"), NSTAT, layer=NSTAT_LAYER, before=1)
        s_dg = Count(sem("rstd_diagonal"), NSTAT, layer=NSTAT_LAYER, before=1)
        s_rb = Count(sem("rstd_spread"), NSTAT, layer=NSTAT_LAYER, before=1)
        s_t = Count(sem("normed"), NSQ, layer=NSQ_LAYER, before=KT)
        s_t_hi = Count(sem("normed_hi"), NSQ, layer=NSQ_LAYER, before=KT)
        s_t_lo = Count(sem("normed_lo"), NSQ, layer=NSQ_LAYER, before=KT)
        s_silu = Count(sem("silu_done"), 0, 4)
        s_gated = Count(sem("gated"), 0, 4)
        s_u_hi = Count(sem("u_hi"), 0, 4)
        s_u_lo = Count(sem("u_lo"), 0, 4)
        s_xf = Count(sem("ffn_added"), 0, 2 * KT)
        LINKS_HALF = NSTAT * RSQRT_LINKS + 3 * 16 + 16
        s_link = Count(sem("vector_chain"), LINKS_HALF, layer=B * LINKS_HALF + 2 * RSQRT_LINKS, before=RSQRT_LINKS)
        s_final = sem("vector_final")
        s_act = sem("scalar_final")
        s_pe = sem("tensor_final")
        s_pre = sem("vector_setup")
        s_prea = sem("scalar_setup")
        s_out = [sem(f"out_stored{n}") for n in range(2)]

        def norm_counts(which, l, b=0):
            if which == "first":
                return (lambda c, j: c.layer_at(l, j)), 0, 0, 0
            if which == "last":
                return (lambda c, j: c.layer_at(l, j)), KT + B * NSQ, KT + B * NADD, 1 + B * NSTAT
            return (lambda c, j: c.half_at(l, b, j)), SQUARES["n"][0], ADDS["n"][0], STATS.index("n")

        def product(pe, out_ap, lhs, rhs, first, last):
            nc.tensor.matmul(out_ap, lhs[0], rhs[0], start=first, stop=False)
            nc.tensor.matmul(out_ap, lhs[0], rhs[1], start=False, stop=False)
            return nc.tensor.matmul(out_ap, lhs[1], rhs[0], start=False, stop=last)

        def rope_target(name):
            if name == "kpe":
                return [kpe], None
            n = int(name[-1])
            if name[0] == "p":
                return [qpe[2 * n], qpe[2 * n + 1]], 2
            return (qd[n % 2], 0) if name[0] == "q" else ([kd[n % 2]], None)

        def plain_target(name):
            n = int(name[2])
            if name[:2] == "vm":
                return [v[s][:, n, :] for s in range(2)]
            return [(qn if name[0] == "q" else kn)[n % 2][s][:] for s in range(2)]

        def normed_target(name, q):
            if name[0] == "y":
                n = int(name[1])
                return [ydiff[s][:, n, :] for s in range(2)], yt(n)
            if name == "ckv":
                return [ckv[s][:] for s in range(2)], t[0][:]
            return [cq[q][s][:] for s in range(2)], t[1 - q][:]

        def yt(n):
            return t[0][:] if n < 3 else sq[0][:]

        block = ctx.enter_context(nc.Block())

        @block.sync
        def _(sp):
            sp.dma_start(cs[:], tables[:, 0:2 * T].rearrange("p (a t) -> p a t", a=2)).then_inc(s_load, 16)
            sp.dma_start(ident[:], tables[:, 2 * T:2 * T + P]).then_inc(s_load, 16)
            sp.dma_start(masks[:], tables[:, 2 * T + P:2 * T + P + 4]).then_inc(s_load, 16)
            sp.dma_start(g[:], gains[:, 0:g.shape[1]]).then_inc(s_load, 16)
            sp.dma_start(gsmall[:], gains[:, g.shape[1]:]).then_inc(s_load, 16)
            sp.dma_start(lamt[:], lam).then_inc(s_load, 16)
            for b in range(B):
                for k in range(0, KT, 2):
                    sp.dma_start(x[:, b, k:k + 2, :], xT[b, :, k:k + 2, :]).then_inc(s_xload, 16)
            with sp.Fori(0, L) as l:
                with sp.Fori(0, B) as b:
                    for j in range(NCH):
                        sp.wait_ge(s_lo.sem, s_lo.half_at(l, b, j - RAW))
                        sp.dma_start(raw[:, j % RAW, :], watt[bass.ds(l * NCH + j, 1), :, :].rearrange(
                            "o p n -> p (o n)")).then_inc(s_raw[j % RAW].sem, 16)
                with sp.Fori(0, FC) as c:
                    for j in range(FCH):
                        sp.wait_ge(s_lo.sem, s_lo.step_at(l, c, j - RAW))
                        sp.dma_start(raw[:, j % RAW, :], wffn[bass.ds(l * (FC * FCH) + c * FCH + j, 1), :, :].rearrange(
                            "o p n -> p (o n)")).then_inc(s_raw[j % RAW].sem, 16)
            for b in range(B):
                for k in range(KT):
                    n = b * KT + k
                    sp.wait_ge(s_final, FINAL_T[n])
                    sp.dma_start(out[b, :, k, :], t[n % 2][:]).then_inc(s_out[n % 2], 16)
            for n in range(2):
                sp.wait_ge(s_out[n], 16 * (B * KT // 2))

        @block.gpsimd
        def _(pool):
            pool.memset(ones[:], 1.0).then_inc(s_pre, 1)
            for c in (s_hi, s_lo):
                pool.sem_inc(c.sem, SEED)

            def split(j, slot, raw_at, hi_at):
                src = raw[:, j % RAW, :]
                pool.wait_ge(s_raw[j % RAW].sem, raw_at)
                nc.gpsimd.tensor_tensor(w[slot][0][:], src, zeros_like(src), ALU.add).then_inc(s_hi.sem, 1)
                pool.wait_ge(s_hi.sem, hi_at)
                nc.gpsimd.tensor_tensor(w[slot][1][:], src, w[slot][0][:].bitcast(F32), ALU.subtract).then_inc(s_lo.sem, 1)

            pool.memset(zero[:], 0.0).then_inc(s_pre, 1)
            pool.wait_ge(s_pre, 2)

            def zeros_like(src):
                return zero[:].to_broadcast([P, CH])

            def ffn_step(l, c, first):
                for j in range(FCH):
                    if first:
                        free = CHUNK_FREE[NCH - WS_ATT + j] if j < WS_ATT else NMM - 1
                        pool.wait_ge(s_mm.sem, s_mm.half_at(l, 1, free))
                    else:
                        pool.wait_ge(s_mm.sem, s_mm.step_at(l, c, FCHUNK_FREE[j] - FMM))
                    split(j, j, s_raw[j % RAW].step_at(l, c, j // RAW), s_hi.step_at(l, c, j))

            with pool.Fori(0, L) as l:
                with pool.Fori(0, B) as b:
                    for j in range(NCH):
                        free = CHUNK_FREE[j - WS_ATT] - (NMM if j < WS_ATT else 0)
                        pool.wait_ge(s_mm.sem, s_mm.half_at(l, b, free))
                        split(j, j % WS_ATT, s_raw[j % RAW].half_at(l, b, j // RAW), s_hi.half_at(l, b, j))
                ffn_step(l, 0, True)
                with pool.Fori(1, FC) as c:
                    ffn_step(l, c, False)

        @block.tensor
        def _(pe):
            for c in (s_mm, s_score, s_tr, s_av, s_st, s_rb):
                pe.sem_inc(c.sem, SEED)

            def sums(wait, done, free):
                pe.wait_ge(*wait)
                pe.wait_ge(*free)
                for m in range(NT):
                    last = nc.tensor.matmul(bank[tail][:, m:m + 1], acc[:, m * P:(m + 1) * P], ones[:, 0:1],
                                            start=True, stop=True)
                last.then_inc(done, 1)

            def spread(wait, done):
                pe.wait_ge(*wait)
                nc.tensor.matmul(bank[tail][:], ones[:], dg[:].rearrange("p m t -> p (m t)"), start=True,
                                 stop=True).then_inc(done, 1)

            def norm_sums(which, l, b=0):
                f, sq0, add0, st0 = norm_counts(which, l, b)
                sums((s_add.sem, f(s_add, add0 + KT - 1)), s_st.sem,
                     (s_t.sem, f(s_t, sq0 - 1)))

            def norm_spread(which, l, b=0):
                f, sq0, add0, st0 = norm_counts(which, l, b)
                spread((s_dg.sem, f(s_dg, st0)), s_rb.sem)

            def chunk(l, b, j):
                pe.wait_ge(s_lo.sem, s_lo.half_at(l, b, j))
                return w[j % WS_ATT]

            def bank_read(l, b, i):
                name = TILES[i] if i >= 0 else TILES[NTILE + i]
                back = 0 if i >= 0 else 1
                for table, count in ((ROPED, s_rope_read), (PLAIN, s_plain_lo), (LATENT, s_latent), (OUTS, s_xo)):
                    if name in table:
                        pe.wait_ge(count.sem, count.half_at(l, b, table[name] - back * len(table)))

            def project(l, b, name, halves):
                i = TILE[name]
                dst = bank[i % 2][:]
                wc = chunk(l, b, chunk_of(name))
                if name[0] in "qk" and name[1].isdigit() or name in ("ckv", "kpe", "cq0", "cq1"):
                    ops = [([wc[s][:, k * P:(k + 1) * P] for s in range(2)], [h0[s][:, k, :] for s in range(2)])
                           for k in range(KT)]
                elif name[:2] == "pe":
                    n = int(name[2])
                    pe.wait_ge(s_t_lo.sem, s_t_lo.half_at(l, b, SQUARES["cq"][1]))
                    ops = [([wc[s][:, k * 2 * P + n * P:k * 2 * P + (n + 1) * P] for s in range(2)],
                            [cq[k][s][:] for s in range(2)]) for k in range(2)]
                elif name[:2] == "qn":
                    n = int(name[2])
                    pe.wait_ge(s_t_lo.sem, s_t_lo.half_at(l, b, SQUARES["cq"][1]))
                    ops = [([wc[s][:, k * 4 * P + n * P:k * 4 * P + (n + 1) * P] for s in range(2)],
                            [cq[k][s][:] for s in range(2)]) for k in range(2)]
                elif name[:2] == "kn":
                    n = int(name[2])
                    pe.wait_ge(s_t_lo.sem, s_t_lo.half_at(l, b, SQUARES["ckv"][0]))
                    ops = [([wc[s][:, n * P:(n + 1) * P] for s in range(2)], [ckv[s][:] for s in range(2)])]
                elif name[:2] == "vm":
                    n = int(name[2])
                    ops = [([ckv[s][:, n * P:(n + 1) * P] for s in range(2)], [wc[s][:, 4 * P:8 * P] for s in range(2)])]
                else:
                    n = int(name[2])
                    y = [[ydiff[s][:, k, :] for s in range(2)] for k in range(H)] if name[1] == "a" else \
                        [[ymla[k][s][:] for s in range(2)] for k in range(H)]
                    ops = [([wc[s][:, k * 2 * P + (n % 2) * P:k * 2 * P + (n % 2 + 1) * P] for s in range(2)], y[k])
                           for k in range(H)]
                    if name[1] == "a":
                        pe.wait_ge(s_t_lo.sem, s_t_lo.half_at(l, b, SQUARES["y3"][0]))
                lo, hi = {"all": (0, len(ops)), "a": (0, len(ops) // 2), "b": (len(ops) // 2, len(ops))}[halves]
                if lo == 0:
                    bank_read(l, b, i - 2)
                for n in range(lo, hi):
                    if name[:2] == "ob" and name[2] == "0" and n == H - 1:
                        pe.wait_ge(s_ym_lo.sem, s_ym_lo.half_at(l, b, H - 1))
                    last = product(pe, dst, ops[n][0], ops[n][1], n == 0, n == len(ops) - 1)
                if hi == len(ops):
                    last.then_inc(s_mm.sem, 1)

            def values(l, b):
                for j in range(4):
                    wc = chunk(l, b, j)
                    if j == 0:
                        pe.wait_ge(s_exp.sem, s_exp.half_at(l, b, -1))
                        pe.wait_ge(s_at_lo.sem, s_at_lo.half_at(l, b, -1))
                    for m in range(NT):
                        for kk in range(2):
                            k = 2 * j + kk
                            last = product(pe, bank[2 + m][:], [h0[s][:, k, m * P:(m + 1) * P] for s in range(2)],
                                           [wc[s][:, kk * 4 * P:(kk + 1) * 4 * P] for s in range(2)], k == 0, k == KT - 1)
                        if j == 3 or m == NT - 1:
                            last.then_inc(s_mm.sem, 1)

            def scores(l, b, i):
                h, qt = i // NT, i % NT
                at_q = slice(qt * P, (qt + 1) * P)
                for c in range(2 if i < 16 else 1):
                    ev = 2 * i + c if i < 16 else 32 + i - 16
                    dst = bank[2 + ev % 3][:]
                    pe.wait_ge(s_exp.sem, s_exp.half_at(l, b, ev - 3))
                    if ev < 3:
                        pe.wait_ge(s_plain_lo.sem, s_plain_lo.half_at(l, b, PLAIN[f"dv{ev}"]))
                    if i < 16:
                        if qt == 0:
                            pe.wait_ge(s_rope_lo.sem, s_rope_lo.half_at(l, b, ROPE_SPLITS[(f"k{h}", 0)]))
                        last = product(pe, dst, [qd[h % 2][c][s][:, at_q] for s in range(2)],
                                       [kd[h % 2][s][:] for s in range(2)], True, True)
                    else:
                        h -= H
                        if qt == 0:
                            pe.wait_ge(s_plain_lo.sem, s_plain_lo.half_at(l, b, PLAIN[f"qn{h}"]))
                            pe.wait_ge(s_rope_lo.sem, s_rope_lo.half_at(l, b, ROPE_SPLITS[(f"pe{h // 2}", h % 2)]))
                        product(pe, dst, [qn[h % 2][s][:, at_q] for s in range(2)], [kn[h % 2][s][:] for s in range(2)],
                                True, False)
                        last = product(pe, dst, [qpe[h][s][:, at_q] for s in range(2)], [kpe[s][:] for s in range(2)],
                                       False, True)
                    last.then_inc(s_score.sem, 1)

            def transposes(l, b, i):
                src = e[2 * i % 4] if i < 16 else e[i % 4]
                pe.wait_ge(s_prob.sem, s_prob.half_at(l, b, i))
                pe.wait_ge(s_at_lo.sem, s_at_lo.half_at(l, b, i - 1))
                if i == 0:
                    pe.wait_ge(s_plain_lo.sem, s_plain_lo.half_at(l, b, PLAIN["dv3"]))
                for k in range(NT):
                    last = nc.tensor.transpose(bank[5][:, k * P:(k + 1) * P], src[:, k * P:(k + 1) * P], ident[:])
                last.then_inc(s_tr.sem, 1)

            def apply_values(l, b, a):
                h, half = a // 2, a % 2
                pe.wait_ge(s_at_lo.sem, s_at_lo.half_at(l, b, 2 * a + 1))
                if half == 0:
                    if h == 0:
                        pe.wait_ge(s_ym_lo.sem, s_ym_lo.half_at(l, b, -1))
                    elif h <= H:
                        pe.wait_ge(s_oc.sem, s_oc.half_at(l, b, h - 1))
                    else:
                        pe.wait_ge(s_ym_lo.sem, s_ym_lo.half_at(l, b, h - H - 1))
                if a == 8:
                    pe.wait_ge(s_plain_lo.sem, s_plain_lo.half_at(l, b, PLAIN["vm3"]))
                dst = bank[6][:, half * 2 * P:(half + 1) * 2 * P]
                for k in range(NT):
                    last = product(pe, dst, [v[s][:, k, (h % H) * P:(h % H + 1) * P] for s in range(2)],
                                   [aT[a % 2][s][:, k, :] for s in range(2)], k == 0, k == NT - 1)
                last.then_inc(s_av.sem, 1)

            pe.wait_ge(s_load, 6 * 16)
            pe.wait_ge(s_pre, PRE_DVE)
            with pe.Fori(0, L) as l:
                pe.wait_ge(s_xf.sem, s_xf.layer_at(l, -1))
                norm_sums("first", l)
                norm_spread("first", l)
                with pe.Fori(0, B) as b:
                    pe.wait_ge(s_t_lo.sem, s_t_lo.half_at(l, b, -1))
                    for step in ORDER:
                        kind = step[0]
                        if kind == "V":
                            values(l, b)
                        elif kind in ("P", "Pa", "Pb"):
                            project(l, b, step[1], {"P": "all", "Pa": "a", "Pb": "b"}[kind])
                        elif kind == "S":
                            scores(l, b, step[1])
                        elif kind == "T":
                            transposes(l, b, step[1])
                        elif kind == "A":
                            apply_values(l, b, step[1])
                        elif kind in ("YD", "ST"):
                            name = f"y{step[1]}" if kind == "YD" else step[1]
                            if name in ("cq", "n"):
                                wait = (s_add.sem, s_add.half_at(l, b, ADDS[name][-1]))
                            else:
                                wait = (s_sq.sem, s_sq.half_at(l, b, SQUARES[name][-1]))
                            sums(wait, s_st.sem, (s_t.sem, s_t.half_at(l, b, SQUARES[name][0] - 1)))
                        elif kind == "RB":
                            spread((s_dg.sem, s_dg.half_at(l, b, STATS.index(step[1]))), s_rb.sem)
                norm_sums("last", l)
                norm_spread("last", l)
                with pe.Fori(0, FC) as c:
                    for tt in range(2):
                        for b in range(B):
                            ev = 2 * tt + b
                            hb = h0 if b == 0 else h1
                            for part in range(2):
                                dst = bank[2 * part + ev % 2][:]
                                j = 2 * tt + part
                                pe.wait_ge(s_lo.sem, s_lo.step_at(l, c, j))
                                if part == 0:
                                    pe.wait_ge(s_silu.sem, s_silu.step_at(l, c, ev - 2))
                                else:
                                    pe.wait_ge(s_gated.sem, s_gated.step_at(l, c, ev - 2))
                                if ev < 2:
                                    if part == 0:
                                        pe.wait_ge(s_xo.sem, s_xo.half_at(l, 1, len(OUTS) - 1))
                                    if part == 1:
                                        pe.wait_ge(s_exp.sem, s_exp.half_at(l, 1, NEV - 1))
                                if b == 1:
                                    pe.wait_ge(s_t_lo.sem, s_t_lo.layer_at(l, NSQ_LAYER - 1))
                                else:
                                    pe.wait_ge(s_t_lo.sem, s_t_lo.half_at(l, 1, NSQ - 1))
                                for k in range(KT):
                                    last = product(pe, dst, [w[j][s][:, k * P:(k + 1) * P] for s in range(2)],
                                                   [hb[s][:, k, :] for s in range(2)], k == 0, k == KT - 1)
                                last.then_inc(s_mm.sem, 1)
                    for b in range(B):
                        for n in range(KT):
                            ev = b * KT + n
                            if n == 0:
                                pe.wait_ge(s_u_lo.sem, s_u_lo.step_at(l, c, 2 + b))
                                if b == 0:
                                    pe.wait_ge(s_lo.sem, s_lo.step_at(l, c, 5))
                            pe.wait_ge(s_xf.sem, s_xf.step_at(l, c, ev - 4))
                            if ev == 0:
                                pe.wait_ge(s_t.sem, s_t.layer_at(l, NSQ_LAYER - 1))
                                pe.wait_ge(s_ym_lo.sem, s_ym_lo.half_at(l, 1, H - 1))
                                pe.wait_ge(s_at_lo.sem, s_at_lo.half_at(l, 1, UNITS - 1))
                            for tt in range(2):
                                last = product(pe, bank[4 + ev % 4][:], [w[4 + tt][s][:, n * P:(n + 1) * P] for s in range(2)],
                                               [u[tt][b][s][:] for s in range(2)], tt == 0, tt == 1)
                            last.then_inc(s_mm.sem, 1)
            for b in range(B):
                pe.wait_ge(s_final, FINAL_ADD[b])
                for m in range(NT):
                    last = nc.tensor.matmul(bank[b][:, m:m + 1], acc[:, m * P:(m + 1) * P], ones[:, 0:1], start=True, stop=True)
                last.then_inc(s_pe, 1)
                pe.wait_ge(s_final, FINAL_DG[b])
                nc.tensor.matmul(bank[b][:], ones[:], dg[:].rearrange("p m t -> p (m t)"), start=True, stop=True).then_inc(s_pe, 1)

        @block.scalar
        def _(act):
            for c in (s_plain_hi, s_rope_hi, s_latent, s_exp, s_at_hi, s_oc, s_ym_hi, s_sq, s_t_hi, s_silu, s_u_hi):
                act.sem_inc(c.sem, SEED)
            act.wait_ge(s_load, 6 * 16)
            act.wait_ge(s_pre, PRE_LAM)
            nc.scalar.activation(rc[:, 0:2 * L], lamv[:, 0:2 * L], ACT.Exp).then_inc(s_prea, 1)
            act.wait_ge(s_xload, 8 * 16)

            def norm_squares(which, l, b=0):
                f, sq0, add0, st0 = norm_counts(which, l, b)
                if which == "first":
                    act.wait_ge(s_xf.sem, s_xf.layer_at(l, -1))
                if which == "tail":
                    act.wait_ge(s_xo.sem, s_xo.half_at(l, b, -1))
                if which == "last":
                    act.wait_ge(s_xo.sem, s_xo.half_at(l, 1, len(OUTS) - 1))
                act.wait_ge(s_t_lo.sem, f(s_t_lo, sq0 - 1))
                for k in range(KT):
                    if k < 2:
                        act.wait_ge(s_st.sem, f(s_st, st0 - 1))
                    else:
                        act.wait_ge(s_add.sem, f(s_add, add0 + k - 2))
                    src = {"first": x[:, 0, k, :], "last": x[:, 1, k, :]}.get(which)
                    if src is None:
                        src = x[:, bass.ds(b * -1 + 1, 1), k, :].rearrange("p o t -> p (o t)")
                    nc.scalar.activation(sq[k % 2][:], src, ACT.Square).then_inc(s_sq.sem, 1)

            def norm_his(which, l, b=0):
                f, sq0, add0, st0 = norm_counts(which, l, b)
                dst = h1 if which == "last" else h0
                if which == "last":
                    act.wait_ge(s_mm.sem, s_mm.half_at(l, 1, NMM - 1))
                for k in range(KT):
                    act.wait_ge(s_t.sem, f(s_t, sq0 + k))
                    nc.scalar.activation(dst[0][:, k, :], t[k % 2][:], ACT.Copy).then_inc(s_t_hi.sem, 1)

            def rope_his(l, b, name):
                dst, scale = rope_target(name)
                act.wait_ge(s_roped.sem, s_roped.half_at(l, b, ROPED[name]))
                for c, d in enumerate(dst):
                    nc.scalar.activation(d[0][:], r1[:], ACT.Copy, scale=1.0 if scale is None else
                                         masks[:, scale + c:scale + c + 1]).then_inc(s_rope_hi.sem, 1)

            def tile_out(l, b, name):
                i = TILE[name]
                src = bank[i % 2][:]
                if name in ROPED:
                    rope_his(l, b, name)
                    return
                if name[0] == "o":
                    return
                act.wait_ge(s_mm.sem, s_mm.half_at(l, b, DV_MM + i))
                if name in LATENT:
                    n = int(name[2]) if name[2].isdigit() else 0
                    stat = "cq" if name[1] == "q" else "ckv"
                    act.wait_ge(s_t_lo.sem, s_t_lo.half_at(l, b, SQUARES["ckv"][0] - (0 if name == "cq1" else 1)))
                    if stat == "ckv":
                        act.wait_ge(s_st.sem, s_st.half_at(l, b, STATS.index(stat) - 1))
                    nc.scalar.activation((acc if stat == "ckv" else sq[n])[:], src, ACT.Square).then_inc(s_sq.sem, 1)
                    nc.scalar.activation(normed_target(stat, n)[1], src, ACT.Copy).then_inc(s_latent.sem, 1)
                else:
                    nc.scalar.activation(plain_target(name)[0], src, ACT.Copy,
                                         scale=MLA_SCALE if name[:2] == "qn" else 1.0).then_inc(s_plain_hi.sem, 1)

            with act.Fori(0, L) as l:
                norm_squares("first", l)
                norm_his("first", l)
                with act.Fori(0, B) as b:
                    for step in ORDER:
                        kind = step[0]
                        if kind == "V":
                            for m in range(NT):
                                act.wait_ge(s_mm.sem, s_mm.half_at(l, b, 3 + m))
                                nc.scalar.activation(v[0][:, m, :], bank[2 + m][:], ACT.Copy).then_inc(s_plain_hi.sem, 1)
                        elif kind in ("P", "Pb"):
                            tile_out(l, b, step[1])
                        elif kind == "S":
                            i = step[1]
                            for c in range(2 if i < 16 else 1):
                                ev = 2 * i + c if i < 16 else 32 + i - 16
                                act.wait_ge(s_max.sem, s_max.half_at(l, b, ev))
                                old = ev - 4 if ev < 4 else (ev - 4) // 2 if ev - 4 < 32 else 16 + ev - 4 - 32
                                act.wait_ge(s_tr.sem, s_tr.half_at(l, b, old))
                                nc.scalar.activation(e[ev % 4][:], bank[2 + ev % 3][:], ACT.Exp, bias=mx[:, ev:ev + 1],
                                                     accum_out=ls[:, ev:ev + 1]).then_inc(s_exp.sem, 1)
                        elif kind == "T":
                            i = step[1]
                            act.wait_ge(s_tr.sem, s_tr.half_at(l, b, i))
                            act.wait_ge(s_av.sem, s_av.half_at(l, b, i // 2 - 2))
                            dst = aT[i // 2 % 2][0][:, :, (i % 2) * P:(i % 2 + 1) * P]
                            nc.scalar.activation(dst, bank[5][:].rearrange("p (k q) -> p k q", k=NT), ACT.Copy).then_inc(s_at_hi.sem, 1)
                        elif kind == "YC":
                            h = step[1]
                            act.wait_ge(s_av.sem, s_av.half_at(l, b, 2 * h + 1))
                            if h < H:
                                n = SQUARES[f"y{h}"][0]
                                act.wait_ge(s_st.sem, s_st.half_at(l, b, STATS.index(f"y{h}") - 1))
                                if h < 3:
                                    act.wait_ge(s_t_lo.sem, s_t_lo.half_at(l, b, n - 1))
                                nc.scalar.activation(acc[:], bank[6][:], ACT.Square).then_inc(s_sq.sem, 1)
                                nc.scalar.activation(yt(h), bank[6][:], ACT.Copy, scale=gsub[:, bass.ds(l, 1)]).then_inc(s_oc.sem, 1)
                            else:
                                nc.scalar.activation(ymla[h - H][0][:], bank[6][:], ACT.Copy).then_inc(s_ym_hi.sem, 1)
                        elif kind == "NQ":
                            norm_squares("tail", l, b)
                        elif kind == "NA":
                            norm_his("tail", l, b)
                        elif kind == "RB" and step[1] != "n":
                            for q, n in enumerate(SQUARES[step[1]]):
                                act.wait_ge(s_t.sem, s_t.half_at(l, b, n))
                                dst, src = normed_target(step[1], q)
                                nc.scalar.activation(dst[0], src, ACT.Copy).then_inc(s_t_hi.sem, 1)
                norm_squares("last", l)
                norm_his("last", l)
                with act.Fori(0, FC) as c:
                    for ev in range(4):
                        tt, b = ev // 2, ev % 2
                        act.wait_ge(s_mm.sem, s_mm.step_at(l, c, 2 * ev))
                        act.wait_ge(s_gated.sem, s_gated.step_at(l, c, ev - 2))
                        if ev == 0:
                            act.wait_ge(s_tr.sem, s_tr.half_at(l, 1, UNITS - 1))
                        nc.scalar.activation(silu[ev % 2][:], bank[ev % 2][:], ACT.Silu).then_inc(s_silu.sem, 1)
                        act.wait_ge(s_gated.sem, s_gated.step_at(l, c, ev))
                        nc.scalar.activation(u[tt][b][0][:], gated[ev % 2][:], ACT.Copy).then_inc(s_u_hi.sem, 1)
            act.wait_ge(s_xf.sem, s_xf.layer_at(L, -1))
            for b in range(B):
                for k in range(KT):
                    n = b * KT + k
                    if FINAL_SQ[n]:
                        act.wait_ge(s_final, FINAL_SQ[n])
                    nc.scalar.activation(sq[k % 2][:], x[:, b, k, :], ACT.Square).then_inc(s_act, 1)

        @block.vector
        def _(dve):
            for c in (s_plain_lo, s_rope_read, s_roped, s_rope_lo, s_xo, s_max, s_prob, s_at_lo, s_ym_lo, s_add, s_dg, s_t,
                      s_t_lo, s_gated, s_u_lo, s_xf, s_link):
                dve.sem_inc(c.sem, SEED)
            pre = [2]

            def setup(ins):
                pre[0] += 1
                ins.then_inc(s_pre, 1)
                dve.wait_ge(s_pre, pre[0])

            dve.wait_ge(s_load, 6 * 16)
            dve.wait_ge(s_pre, 2)
            setup(nc.vector.tensor_tensor(e[1][:, 0:4 * DH], lamt[:, 0:4 * DH], lamt[:, 4 * DH:8 * DH], ALU.mult))
            setup(nc.vector.tensor_reduce(lamv[:], e[1][:, 0:4 * DH].rearrange("p (a d) -> p a d", a=4), AX_X, ALU.add))
            assert pre[0] == PRE_LAM
            dve.wait_ge(s_prea, 1)
            for l in range(L):
                setup(nc.vector.tensor_tensor(lamv[:, 2 * l + 1:2 * l + 2], rc[:, 2 * l + 1:2 * l + 2], rc[:, 2 * l:2 * l + 1],
                                              ALU.subtract))
                setup(nc.vector.tensor_scalar(lamv[:, 2 * l + 1:2 * l + 2], lamv[:, 2 * l + 1:2 * l + 2], -LAM_INIT[l], None,
                                              ALU.add))
                setup(nc.vector.memset(lamv[:, 2 * l:2 * l + 1], 1.0))
                setup(nc.vector.tensor_scalar(gsub[:, l:l + 1], gsmall[:, 4 * l:4 * l + 1], 1.0 - LAM_INIT[l], None, ALU.mult))
            assert pre[0] == PRE_DVE

            def rsqrt_diagonal(link, width, src, wait, done):
                dve.wait_ge(*wait)
                var = ms[0][:]
                a = ms[1][:]
                link(nc.vector.tensor_scalar(var, src, 1.0 / width, EPS, ALU.mult, ALU.add))
                link(nc.vector.tensor_scalar(yi[:], var.bitcast(I32), 1, None, ALU.logical_shift_right))
                link(nc.vector.tensor_scalar(yy[:].bitcast(I32), yi[:], -1.0, float(0x5F3759DF), ALU.mult, ALU.add))
                for _ in range(3):
                    link(nc.vector.tensor_tensor(a, yy[:], yy[:], ALU.mult))
                    link(nc.vector.scalar_tensor_tensor(a, a, -0.5, var, ALU.mult, ALU.mult))
                    link(nc.vector.scalar_tensor_tensor(yy[:], a, 1.5, yy[:], ALU.add, ALU.mult))
                nc.vector.tensor_tensor(dg[:], ident[:].unsqueeze(1).to_broadcast([P, NT, P]),
                                        yy[:].unsqueeze(2).to_broadcast([P, NT, P]), ALU.mult).then_inc(done, 1)

            def chain(value):
                n = [0]

                def link(ins):
                    ins.then_inc(s_link.sem, 1)
                    dve.wait_ge(s_link.sem, value(n[0]))
                    n[0] += 1
                return link, n

            def norm(which, l, b, part, link):
                f, sq0, add0, st0 = norm_counts(which, l, b)
                if part == "add":
                    for k in range(KT):
                        dve.wait_ge(s_sq.sem, f(s_sq, sq0 + k))
                        if k == 0:
                            dve.wait_ge(s_st.sem, f(s_st, st0 - 1))
                            nc.vector.tensor_copy(acc[:], sq[0][:]).then_inc(s_add.sem, 1)
                        else:
                            dve.wait_ge(s_add.sem, f(s_add, add0 + k - 1))
                            nc.vector.tensor_tensor(acc[:], acc[:], sq[k % 2][:], ALU.add).then_inc(s_add.sem, 1)
                if part == "rsqrt":
                    dve.wait_ge(s_rb.sem, f(s_rb, st0 - 1))
                    rsqrt_diagonal(link, D, bank[tail][:, 0:NT], (s_st.sem, f(s_st, st0)), s_dg.sem)
                if part == "apply":
                    dst = h1 if which == "last" else h0
                    dve.wait_ge(s_rb.sem, f(s_rb, st0))
                    for k in range(KT + 1):
                        if k < KT:
                            if which == "tail":
                                xk = x[:, bass.ds(b * -1 + 1, 1), k, :].rearrange("p o t -> p (o t)")
                                gk = g[:, bass.ds(l * (4 * KT) + b * KT + (KT + k), 1)]
                            else:
                                n = 0 if which == "first" else 3
                                xk = x[:, 0 if which == "first" else 1, k, :]
                                gk = g[:, bass.ds(l * (4 * KT) + n * KT + k, 1)]
                            dve.wait_ge(s_t_lo.sem, f(s_t_lo, sq0 + k - 2))
                            nc.vector.scalar_tensor_tensor(t[k % 2][:], xk, gk, bank[tail][:], ALU.mult,
                                                           ALU.mult).then_inc(s_t.sem, 1)
                        if k > 0:
                            dve.wait_ge(s_t_hi.sem, f(s_t_hi, sq0 + k - 1))
                            nc.vector.tensor_tensor(dst[1][:, k - 1, :], t[(k - 1) % 2][:], dst[0][:, k - 1, :].bitcast(F32),
                                                    ALU.subtract).then_inc(s_t_lo.sem, 1)

            def rope(l, b, name):
                i = TILE[name]
                z = bank[i % 2]
                dve.wait_ge(s_mm.sem, s_mm.half_at(l, b, DV_MM + i))
                q0 = min(n for (tn, c), n in ROPE_SPLITS.items() if tn == name)
                dve.wait_ge(s_rope_lo.sem, s_rope_lo.half_at(l, b, q0 - 1))
                nc.vector.tensor_tensor(r1[:], z[:], cs[:, 0, :], ALU.mult)
                nc.vector.tensor_tensor(r2[0:64, :], z[64:128, :], cs[64:128, 1, :], ALU.mult)
                nc.vector.tensor_tensor(r2[64:128, :], z[0:64, :], cs[0:64, 1, :], ALU.mult).then_inc(s_rope_read.sem, 1)
                dve.wait_ge(s_rope_read.sem, s_rope_read.half_at(l, b, ROPED[name]))
                nc.vector.tensor_tensor(r1[:], r1[:], r2[:], ALU.add).then_inc(s_roped.sem, 1)
                dst, scale = rope_target(name)
                for c, d in enumerate(dst):
                    dve.wait_ge(s_rope_hi.sem, s_rope_hi.half_at(l, b, q0 + c))
                    if scale is None:
                        last = nc.vector.tensor_tensor(d[1][:], r1[:], d[0][:].bitcast(F32), ALU.subtract)
                    else:
                        last = nc.vector.scalar_tensor_tensor(d[1][:], r1[:], masks[:, scale + c:scale + c + 1],
                                                              d[0][:].bitcast(F32), ALU.mult, ALU.subtract)
                    last.then_inc(s_rope_lo.sem, 1)

            def tile_out(l, b, name):
                i = TILE[name]
                src = bank[i % 2][:]
                if name in ROPED:
                    rope(l, b, name)
                elif name[0] == "o":
                    n = int(name[2])
                    dve.wait_ge(s_mm.sem, s_mm.half_at(l, b, DV_MM + i))
                    if name[1] == "b":
                        dve.wait_ge(s_xo.sem, s_xo.half_at(l, b, OUTS[f"oa{n}"]))
                    xn = x[:, bass.ds(b, 1), n, :].rearrange("p o t -> p (o t)")
                    nc.vector.tensor_tensor(xn, xn, src, ALU.add).then_inc(s_xo.sem, 1)
                elif name in PLAIN:
                    hi, lo = plain_target(name)
                    dve.wait_ge(s_plain_hi.sem, s_plain_hi.half_at(l, b, PLAIN[name]))
                    if name[:2] == "qn":
                        last = nc.vector.scalar_tensor_tensor(lo, src, MLA_SCALE, hi.bitcast(F32), ALU.mult, ALU.subtract)
                    else:
                        last = nc.vector.tensor_tensor(lo, src, hi.bitcast(F32), ALU.subtract)
                    last.then_inc(s_plain_lo.sem, 1)
                elif name == "cq1":
                    dve.wait_ge(s_sq.sem, s_sq.half_at(l, b, SQUARES["cq"][1]))
                    nc.vector.tensor_tensor(acc[:], sq[0][:], sq[1][:], ALU.add).then_inc(s_add.sem, 1)

            def stat_rsqrt(l, b, name, link):
                n = STATS.index(name)
                dve.wait_ge(s_rb.sem, s_rb.half_at(l, b, n - 1))
                width = {"ckv": KVL, "cq": QL}.get(name, P)
                rsqrt_diagonal(link, width, bank[tail][:, 0:NT], (s_st.sem, s_st.half_at(l, b, n)), s_dg.sem)

            def stat_apply(l, b, name):
                dve.wait_ge(s_rb.sem, s_rb.half_at(l, b, STATS.index(name)))
                for q, n in enumerate(SQUARES[name]):
                    dst, src = normed_target(name, q)
                    if name[0] == "y":
                        dve.wait_ge(s_oc.sem, s_oc.half_at(l, b, int(name[1])))
                        nc.vector.tensor_tensor(src, src, bank[tail][:], ALU.mult).then_inc(s_t.sem, 1)
                    else:
                        dve.wait_ge(s_latent.sem, s_latent.half_at(l, b, LATENT["ckv" if name == "ckv" else f"cq{q}"]))
                        o = 3 if name == "ckv" else 1 + q
                        nc.vector.scalar_tensor_tensor(src, src, gsmall[:, bass.ds(l * 4 + o, 1)], bank[tail][:], ALU.mult,
                                                       ALU.mult).then_inc(s_t.sem, 1)
                for q, n in enumerate(SQUARES[name]):
                    dst, src = normed_target(name, q)
                    dve.wait_ge(s_t_hi.sem, s_t_hi.half_at(l, b, n))
                    nc.vector.tensor_tensor(dst[1], src, dst[0].bitcast(F32), ALU.subtract).then_inc(s_t_lo.sem, 1)

            def combine(l, b, i, link):
                evs = [2 * i, 2 * i + 1] if i < 16 else [32 + i - 16]
                dve.wait_ge(s_exp.sem, s_exp.half_at(l, b, evs[-1]))
                if i < 16:
                    link(nc.vector.reciprocal(rc[:, 0:2], ls[:, evs[0]:evs[1] + 1]))
                    link(nc.vector.tensor_tensor(rc[:, 2:4], rc[:, 0:2], lamv[:, bass.ds(l * 2, 2)], ALU.mult))
                    p0, p1 = e[evs[0] % 4][:], e[evs[1] % 4][:]
                    link(nc.vector.tensor_scalar(p0, p0, rc[:, 2:3], None, ALU.mult))
                    nc.vector.scalar_tensor_tensor(p0, p1, rc[:, 3:4], p0, ALU.mult, ALU.add).then_inc(s_prob.sem, 1)
                else:
                    link(nc.vector.reciprocal(rc[:, 0:1], ls[:, evs[0]:evs[0] + 1]))
                    p0 = e[evs[0] % 4][:]
                    nc.vector.tensor_scalar(p0, p0, rc[:, 0:1], None, ALU.mult).then_inc(s_prob.sem, 1)

            with dve.Fori(0, L) as l:
                link, n = chain(lambda j: s_link.layer_at(l, j))
                norm("first", l, 0, "add", link)
                norm("first", l, 0, "rsqrt", link)
                norm("first", l, 0, "apply", link)
                assert n[0] == RSQRT_LINKS, n
                with dve.Fori(0, B) as b:
                    link, n = chain(lambda j: s_link.half_at(l, b, j))
                    for step in ORDER:
                        kind = step[0]
                        if kind == "V":
                            for m in range(NT):
                                dve.wait_ge(s_plain_hi.sem, s_plain_hi.half_at(l, b, m))
                                nc.vector.tensor_tensor(v[1][:, m, :], bank[2 + m][:], v[0][:, m, :].bitcast(F32),
                                                        ALU.subtract).then_inc(s_plain_lo.sem, 1)
                        elif kind in ("P", "Pb"):
                            tile_out(l, b, step[1])
                        elif kind == "S":
                            i = step[1]
                            evs = [2 * i, 2 * i + 1] if i < 16 else [32 + i - 16]
                            for ev in evs:
                                dve.wait_ge(s_score.sem, s_score.half_at(l, b, ev))
                                nc.vector.tensor_reduce(mx[:, ev:ev + 1], bank[2 + ev % 3][:], AX_X, ALU.max,
                                                        negate=True).then_inc(s_max.sem, 1)
                            if i not in (0, 16):
                                combine(l, b, i - 1, link)
                        elif kind == "T":
                            i = step[1]
                            if i in (15, 31):
                                combine(l, b, i, link)
                            dve.wait_ge(s_at_hi.sem, s_at_hi.half_at(l, b, i))
                            q = slice((i % 2) * P, (i % 2 + 1) * P)
                            nc.vector.tensor_tensor(aT[i // 2 % 2][1][:, :, q], bank[5][:].rearrange("p (k q) -> p k q", k=NT),
                                                    aT[i // 2 % 2][0][:, :, q].bitcast(F32), ALU.subtract).then_inc(s_at_lo.sem, 1)
                        elif kind == "YC" and step[1] >= H:
                            h = step[1] - H
                            dve.wait_ge(s_ym_hi.sem, s_ym_hi.half_at(l, b, h))
                            nc.vector.tensor_tensor(ymla[h][1][:], bank[6][:], ymla[h][0][:].bitcast(F32),
                                                    ALU.subtract).then_inc(s_ym_lo.sem, 1)
                        elif kind == "NQ":
                            norm("tail", l, b, "add", link)
                        elif kind == "ST" and step[1] == "n":
                            norm("tail", l, b, "rsqrt", link)
                        elif kind == "NA":
                            norm("tail", l, b, "apply", link)
                        elif kind in ("ST", "YD"):
                            stat_rsqrt(l, b, f"y{step[1]}" if kind == "YD" else step[1], link)
                        elif kind == "RB" and step[1] != "n":
                            stat_apply(l, b, step[1])
                    assert n[0] == LINKS_HALF, (n, LINKS_HALF)
                link, n = chain(lambda j: s_link.layer_at(l, RSQRT_LINKS + B * LINKS_HALF + j))
                norm("last", l, 0, "add", link)
                norm("last", l, 0, "rsqrt", link)
                norm("last", l, 0, "apply", link)
                with dve.Fori(0, FC) as c:
                    for ev in range(4):
                        tt, b = ev // 2, ev % 2
                        dve.wait_ge(s_silu.sem, s_silu.step_at(l, c, ev))
                        dve.wait_ge(s_mm.sem, s_mm.step_at(l, c, 2 * ev + 1))
                        dve.wait_ge(s_u_lo.sem, s_u_lo.step_at(l, c, ev - 2))
                        nc.vector.tensor_tensor(gated[ev % 2][:], bank[2 + ev % 2][:], silu[ev % 2][:], ALU.mult).then_inc(s_gated.sem, 1)
                        dve.wait_ge(s_u_hi.sem, s_u_hi.step_at(l, c, ev))
                        nc.vector.tensor_tensor(u[tt][b][1][:], gated[ev % 2][:], u[tt][b][0][:].bitcast(F32),
                                                ALU.subtract).then_inc(s_u_lo.sem, 1)
                    for b in range(B):
                        for n in range(KT):
                            ev = b * KT + n
                            dve.wait_ge(s_mm.sem, s_mm.step_at(l, c, 8 + ev))
                            dve.wait_ge(s_xf.sem, s_xf.step_at(l, c, ev - 2 * KT))
                            nc.vector.tensor_tensor(x[:, b, n, :], x[:, b, n, :], bank[4 + ev % 4][:], ALU.add).then_inc(s_xf.sem, 1)
            n = [0]

            def final(ins):
                ins.then_inc(s_final, 1)
                n[0] += 1
                dve.wait_ge(s_final, n[0])

            for b in range(B):
                for k in range(KT):
                    assert n[0] >= FINAL_SQ[b * KT + k]
                    dve.wait_ge(s_act, b * KT + k + 1)
                    if k == 0:
                        if b:
                            dve.wait_ge(s_pe, 2 * b)
                        final(nc.vector.tensor_copy(acc[:], sq[0][:]))
                    else:
                        final(nc.vector.tensor_tensor(acc[:], acc[:], sq[k % 2][:], ALU.add))
                assert n[0] == FINAL_ADD[b]
                rsqrt_diagonal(final, D, bank[b][:, 0:NT], (s_pe, 2 * b + 1), s_final)
                n[0] += 1
                assert n[0] == FINAL_DG[b]
                dve.wait_ge(s_pe, 2 * b + 2)
                for k in range(KT):
                    m = b * KT + k
                    if m >= 2:
                        dve.wait_ge(s_out[m % 2], 16 * (m // 2))
                    final(nc.vector.scalar_tensor_tensor(t[m % 2][:], x[:, b, k, :], g[:, 4 * L * KT + k:4 * L * KT + k + 1],
                                                         bank[b][:], ALU.mult, ALU.mult))
                    assert n[0] == FINAL_T[m]


def _tile(w, cols):
    a = w[:, cols]
    return a.reshape(-1, P, len(cols)).transpose(1, 0, 2).reshape(P, -1)


def _pair(base0, base1):
    half = np.arange(DH // 2)
    return np.concatenate([base0 + half, base1 + half, base0 + DH // 2 + half, base1 + DH // 2 + half])


def _attention_chunks(w_in, w_q_b, w_kv_b, w_o):
    width = H * 2 * DH
    parts = []
    for name in CHUNKS:
        if name[:2] == "dv":
            j = int(name[2])
            a = _tile(w_in[2 * j * P:2 * (j + 1) * P], np.arange(2 * width, 3 * width))
        elif name[0] in "qk" and name[1].isdigit():
            h = int(name[1])
            base = (width if name[0] == "k" else 0) + 2 * h * DH
            a = _tile(w_in, _pair(base, base + DH))
        elif name == "kpe":
            base = 3 * width + QL + KVL
            a = _tile(w_in, _pair(base, base))
        elif name == "ckv":
            a = _tile(w_in, 3 * width + QL + np.arange(KVL))
        elif name[:2] == "cq":
            a = _tile(w_in, 3 * width + int(name[2]) * P + np.arange(P))
        elif name == "pe":
            base = [h * (NOPE + ROPE) + NOPE for h in range(H)]
            a = _tile(w_q_b, np.concatenate([_pair(base[0], base[1]), _pair(base[2], base[3])]))
        elif name == "qn":
            a = _tile(w_q_b, np.concatenate([h * (NOPE + ROPE) + np.arange(NOPE) for h in range(H)]))
        elif name == "kvb":
            a = _tile(w_kv_b, np.concatenate([h * 2 * P + s * P + np.arange(P) for s in range(2) for h in range(H)]))
        else:
            rows = 0 if name[1] == "a" else H * P
            a = _tile(w_o[rows:rows + H * P], int(name[2]) * 2 * P + np.arange(2 * P))
        out = np.zeros((P, CH), w_in.dtype)
        out[:, :a.shape[1]] = a
        parts.append(out)
    return np.stack(parts)


def _ffn_chunks(w_gate, w_up, w_down):
    parts = []
    for c in range(FC):
        for f in (2 * c, 2 * c + 1):
            parts += [_tile(w_gate, f * P + np.arange(P)), _tile(w_up, f * P + np.arange(P))]
        for f in (2 * c, 2 * c + 1):
            parts.append(w_down[f * P:(f + 1) * P])
    return np.stack(parts)


def _tables():
    half = DH // 2
    inv = (1.0 / (np.float32(10000.0) ** (np.arange(half, dtype=np.float32) * np.float32(2.0) / np.float32(DH)))).astype(np.float32)
    ang = (np.arange(T, dtype=np.float32)[None, :] * inv[:, None]).astype(np.float32)
    cos = np.tile(np.cos(ang.astype(np.float64)), (4, 1))
    sin = np.tile(np.sin(ang.astype(np.float64)), (4, 1))
    sin[2 * half:] *= -1
    masks = np.zeros((P, 4))
    for c in range(2):
        rows = (np.arange(P) // half) % 2 == c
        masks[rows, c] = DIFF_SCALE
        masks[rows, 2 + c] = MLA_SCALE
    return np.concatenate([cos, sin, np.eye(P), masks], axis=1).astype(np.float32)


def kernel(x_prompt, x_sample, attn_norm, w_in, lam_q1, lam_k1, lam_q2, lam_k2, diff_subln, q_a_norm, w_q_b, kv_a_norm,
           w_kv_b, w_o, ffn_norm, w_gate, w_up, w_down, final_norm):
    import concourse.bacc as bacc
    from concourse.bass_utils import run_bass_kernel_spmd

    def features(a):
        return np.ascontiguousarray(a.T.reshape(-1, P, a.shape[0]).transpose(1, 0, 2))

    a = {k: np.asarray(val) for k, val in dict(
        x_prompt=x_prompt, x_sample=x_sample, attn_norm=attn_norm, w_in=w_in, lam_q1=lam_q1, lam_k1=lam_k1, lam_q2=lam_q2,
        lam_k2=lam_k2, diff_subln=diff_subln, q_a_norm=q_a_norm, w_q_b=w_q_b, kv_a_norm=kv_a_norm, w_kv_b=w_kv_b, w_o=w_o,
        ffn_norm=ffn_norm, w_gate=w_gate, w_up=w_up, w_down=w_down, final_norm=final_norm).items()}
    by_tile = lambda v: v.reshape(-1, P).T
    gains = [by_tile(a[n][l]) for l in range(L) for n in ("attn_norm", "attn_norm", "ffn_norm", "ffn_norm")]
    gains.append(by_tile(a["final_norm"]))
    for l in range(L):
        gains += [by_tile(a["diff_subln"][l]), by_tile(a["q_a_norm"][l]), by_tile(a["kv_a_norm"][l])]
    lam = [a[n][l] for pair in (("lam_q1", "lam_q2"), ("lam_k1", "lam_k2")) for l in range(L) for n in pair]
    arrays = {
        "xT": np.stack([features(a["x_prompt"][0]), features(a["x_sample"][0])]),
        "watt": np.concatenate([_attention_chunks(a["w_in"][l], a["w_q_b"][l], a["w_kv_b"][l], a["w_o"][l]) for l in range(L)]),
        "wffn": np.concatenate([_ffn_chunks(a["w_gate"][l], a["w_up"][l], a["w_down"][l]) for l in range(L)]),
        "tables": _tables(),
        "gains": np.ascontiguousarray(np.concatenate(gains, axis=1)),
        "lam": np.ascontiguousarray(np.broadcast_to(np.concatenate(lam)[None, :], (P, 8 * DH))),
    }
    nc = bacc.Bacc("TRN2", target_bir_lowering=False, num_devices=1)
    args = [nc.dram_tensor(f"in_{n}", v.shape, F32, kind="ExternalInput").ap() for n, v in arrays.items()]
    out = nc.dram_tensor("out_yT", (B, P, KT, T), F32, kind="ExternalOutput").ap()
    encoder_trunk(nc, *args, out)
    r = run_bass_kernel_spmd(nc, [{f"in_{n}": v for n, v in arrays.items()}], core_ids=[0])
    y = r.results[0]["out_yT"]
    return tuple(np.ascontiguousarray(y[b].transpose(2, 1, 0).reshape(1, T, D)) for b in range(B))
```

```python
from contextlib import ExitStack
import math

import numpy as np

import concourse.bass as bass
from concourse import mybir
from concourse.alu_op_type import AluOpType as ALU

ACT = mybir.ActivationFunctionType
F32 = mybir.dt.float32
F32R = mybir.dt.float32r
I32 = mybir.dt.int32
AX_X = mybir.AxisListType.X

P = 128
D = 1024
KT = D // P
T = 512
NT = T // P
L = 2
B = 2
H = 4
DH = 64
ROPE = 64
NOPE = 128
QL = 256
KVL = 128
FF = 2816
FT = FF // P
FC = FT // 2
CH = 1024
EPS = 1e-6
DIFF_SCALE = DH ** -0.5
MLA_SCALE = (NOPE + ROPE) ** -0.5
LAM_INIT = [0.8 - 0.6 * math.exp(-0.3 * l) for l in range(L)]
SEED = 64

CHUNKS = ([f"dv{j}" for j in range(4)] + [f"{x}{h}" for h in range(H) for x in "qk"]
          + ["kpe", "ckv", "cq0", "cq1", "pe", "qn", "kvb"]
          + [f"oa{j}" for j in range(4)] + [f"ob{j}" for j in range(4)])
NCH = len(CHUNKS)
FCH = 6
RAW = 3
WS_ATT = 3
WS_FFN = 6
assert NCH % RAW == 0 and NCH % WS_ATT == 0 and FCH % RAW == 0 and FCH % WS_FFN == 0
CHUNKS_LAYER = B * NCH + FC * FCH

UNITS = 2 * H * NT



def order(text):
    return [tuple(int(w) if w.isdigit() else w for w in item.split()) for item in text.split("|")]


TENSOR_ORDER = order("""
    V | P q0 | P k0 | P q1 | S 0 | Pa k1 | S 1 | Pb k1 | T 0 | S 2 | Pa q2 | T 1 | Pb q2 | A 0 | S 3 | T 2 | S 4 |
    Pa k2 | T 3 | S 5 | Pb k2 | A 1 | T 4 | Pa q3 | S 6 | ST y0 | T 5 | S 7 | RB y0 | Pb q3 | A 2 | T 6 | S 8 |
    Pa k3 | T 7 | S 9 | Pb k3 | A 3 | T 8 | S 10 | ST y1 | P ckv | T 9 | S 11 | RB y1 | P kpe | A 4 | T 10 | S 12 |
    ST ckv | P cq0 | T 11 | S 13 | RB ckv | P cq1 | A 5 | T 12 | S 14 | P kn0 | ST cq | T 13 | S 15 | RB cq | A 6 |
    T 14 | P pe0 | P qn0 | P pe1 | T 15 | S 16 | ST y2 | A 7 | P vm0 | P vm1 | S 17 | RB y2 | P vm2 | T 16 | S 18 |
    P vm3 | ST y3 | P kn1 | P qn1 | T 17 | S 19 | RB y3 | A 8 | T 18 | S 20 | P oa0 | T 19 | S 21 | A 9 | P oa1 |
    T 20 | S 22 | P kn2 | P qn2 | T 21 | S 23 | T 22 | S 24 | P kn3 | P qn3 | T 23 | A 10 | S 25 | ST n | A 11 |
    S 26 | P oa2 | T 24 | RB n | P oa3 | T 25 | S 27 | A 12 | P oa4 | T 26 | S 28 | P oa5 | T 27 | S 29 | A 13 |
    T 28 | S 30 | T 29 | P oa6 | S 31 | A 14 | T 30 | P oa7 | T 31 | Pa ob0 | A 15 | Pa ob1 | Pb ob0 | Pb ob1 |
    P ob2 | P ob3 | P ob4 | P ob5 | P ob6 | P ob7
""")
SCALAR_ORDER = order("""
    V | RH q0 | RH k0 | EX 0 | RH q1 | EX 1 | TH 0 | EX 2 | TH 1 | RH k1 | EX 3 | TH 2 | EX 4 | TH 3 | RH q2 | TH 4
    | EX 5 | YC 0 | EX 6 | TH 5 | RH k2 | EX 7 | TH 6 | SH y0 | EX 8 | TH 7 | RH q3 | EX 9 | YC 1 | TH 8 | EX 10 |
    TH 9 | RH k3 | EX 11 | TH 10 | SH y1 | LC ckv | EX 12 | TH 11 | EX 13 | RH kpe | YC 2 | TH 12 | SH ckv | LC cq0
    | LC cq1 | EX 14 | TH 13 | PH kn0 | EX 15 | TH 14 | SH cq | PH qn0 | RH pe0 | TH 15 | RH pe1 | PH vm0 | EX 16 |
    PH vm1 | EX 17 | YC 3 | TH 16 | SH y2 | PH vm2 | PH vm3 | EX 18 | TH 17 | PH kn1 | PH qn1 | EX 19 | TH 18 |
    SH y3 | EX 20 | TH 19 | EX 21 | SQ 0 | SQ 1 | YC 4 | TH 20 | SQ 2 | SQ 3 | EX 22 | TH 21 | PH kn2 | PH qn2 |
    SQ 4 | EX 23 | TH 22 | SQ 5 | SQ 6 | SQ 7 | EX 24 | TH 23 | PH kn3 | PH qn3 | EX 25 | YC 5 | TH 24 | EX 26 |
    TH 25 | EX 27 | TH 26 | EX 28 | TH 27 | EX 29 | YC 6 | TH 28 | EX 30 | TH 29 | EX 31 | TH 30 | TH 31 | SN 0 |
    SN 1 | YC 7 | SN 2 | SN 3 | SN 4 | SN 5 | SN 6 | SN 7
""")
VECTOR_ORDER = order("""
    V | RP q0 | RL q0 | RP k0 | RL k0 | MX 0 | RP q1 | CB 0 | MX 1 | RL q1 | CB 1 | TL 0 | MX 2 | RP k1 | TL 1 |
    CB 2 | MX 3 | RL k1 | TL 2 | CB 3 | MX 4 | RP q2 | TL 3 | CB 4 | MX 5 | RL q2 | TL 4 | CB 5 | MX 6 | RQ y0 |
    RP k2 | CB 6 | TL 5 | MX 7 | AP y0 | RL k2 | CB 7 | TL 6 | MX 8 | AL y0 | RP q3 | TL 7 | CB 8 | MX 9 | RL q3 |
    TL 8 | CB 9 | MX 10 | RQ y1 | RP k3 | TL 9 | AP y1 | MX 11 | RL k3 | CB 10 | TL 10 | CB 11 | MX 12 | AL y1 |
    RQ ckv | RP kpe | AP ckv | CB 12 | MX 13 | TL 11 | RL kpe | TL 12 | AL ckv | CB 13 | MX 14 | RQ cq | TL 13 |
    CB 14 | MX 15 | PL kn0 | AP cq | AL cq | TL 14 | CB 15 | RP pe0 | PL qn0 | RL pe0 | TL 15 | MX 16 | RP pe1 |
    RQ y2 | PL vm0 | PL vm1 | CB 16 | MX 17 | RL pe1 | AP y2 | PL vm2 | TL 16 | PL vm3 | CB 17 | MX 18 | AL y2 |
    RQ y3 | TL 17 | CB 18 | MX 19 | PL kn1 | PL qn1 | AP y3 | TL 18 | AL y3 | CB 19 | MX 20 | TL 19 | CB 20 | XO oa0
    | MX 21 | TL 20 | XO oa1 | CB 21 | MX 22 | TL 21 | CB 22 | MX 23 | PL kn2 | YL 4 | PL qn2 | TL 22 | CB 23 |
    MX 24 | TL 23 | CB 24 | MX 25 | PL kn3 | PL qn3 | RQ n | CB 25 | MX 26 | XO oa2 | YL 5 | TL 24 | TL 25 | CB 26 |
    MX 27 | XO oa3 | XO oa4 | TL 26 | MX 28 | CB 27 | TL 27 | CB 28 | MX 29 | XO oa5 | TL 28 | CB 29 | MX 30 | YL 6
    | XO oa6 | TL 29 | CB 30 | MX 31 | CB 31 | TL 30 | XO oa7 | AN 0 | AN 1 | TL 31 | AN 2 | LN 0 | AN 3 | YL 7 |
    LN 1 | XO ob0 | AN 4 | XO ob1 | LN 2 | AN 5 | LN 3 | LN 4 | XO ob2 | AN 6 | XO ob3 | AN 7 | LN 5 | LN 6 | LN 7 |
    XO ob4 | XO ob5 | XO ob6 | XO ob7
""")

STATS = [s[1] for s in TENSOR_ORDER if s[0] == "RB"]
NSTAT = len(STATS)
TILES = []
for _s in TENSOR_ORDER:
    if _s[0] in ("P", "Pa"):
        TILES.append(_s[1])
TILE = {n: i for i, n in enumerate(TILES)}
NTILE = len(TILES)
assert NTILE == 42 and NTILE % 2 == 0 and NSTAT == 7


def numbered(names):
    return {n: i for i, n in enumerate(names)}


DV_MM = 7
ROPED = numbered([s[1] for s in VECTOR_ORDER if s[0] == "RP"])
ROPE_SPLITS = numbered([(n, c) for n in ROPED for c in range(2 if n[0] in "qp" else 1)])
PLAIN = numbered(["dv0", "dv1", "dv2", "dv3"] + [s[1] for s in VECTOR_ORDER if s[0] == "PL"])
LATENT = numbered([s[1] for s in SCALAR_ORDER if s[0] == "LC"])
OUTS = numbered([s[1] for s in VECTOR_ORDER if s[0] == "XO"])
SQUARED = numbered([(f"y{s[1]}", 0) if s[0] == "YC" else ("ckv", 0) if s[1] == "ckv" else ("cq", int(s[1][2])) if s[0] == "LC"
                    else ("n", s[1]) for s in SCALAR_ORDER if s[0] in ("LC", "SQ") or s[0] == "YC" and s[1] < H])
SQUARES = {}
for _s in STATS:
    _n = {"n": KT, "cq": 2}.get(_s, 1)
    _at = sum(len(v) for v in SQUARES.values())
    SQUARES[_s] = list(range(_at, _at + _n))
NSQ = sum(len(v) for v in SQUARES.values())
NSQ_LAYER = B * NSQ + 2 * KT
NADD = KT
NADD_LAYER = B * NADD + 2 * KT
NSTAT_LAYER = B * NSTAT + 2
NEV = 2 * 16 + 16
RSQRT_LINKS = 12


def chunk_of(tile):
    if tile in ("pe0", "pe1"):
        return CHUNKS.index("pe")
    if tile[:2] == "qn":
        return CHUNKS.index("qn")
    if tile[:2] in ("kn", "vm"):
        return CHUNKS.index("kvb")
    if tile[0] == "o":
        return CHUNKS.index(tile[:2] + str(int(tile[2]) // 2))
    return CHUNKS.index(tile)


CHUNK_FREE = [0, 1, 2, 6] + [DV_MM + max(TILE[t] for t in TILES if chunk_of(t) == j) for j in range(4, NCH)]
NMM = DV_MM + NTILE
FMM = 8 + 2 * KT
FCHUNK_FREE = [2, 3, 6, 7, FMM - 1, FMM - 1]
PRE_LAM = 4
PRE_DVE = PRE_LAM + 4 * L
FINAL_ADD = KT
FINAL_DG = KT + 4 + RSQRT_LINKS + 1
FINAL_T = [KT + n + 1 if n < 4 else FINAL_DG + n - 3 for n in range(B * KT)]


def e_buffer(ev):
    return ev % 6 if ev < 32 else (ev + 2) % 6


def e_before(ev):
    unit = lambda x: x // 2 if x < 32 else x - 16
    old = [x for x in range(ev) if e_buffer(x) == e_buffer(ev)]
    return unit(old[-1]) if old else unit(max(x for x in range(NEV) if e_buffer(x) == e_buffer(ev))) - UNITS


class Count:

    def __init__(self, sem, half=0, step=0, layer=None, seed=SEED, before=0, unit=1):
        self.sem, self.half, self.step, self.seed, self.before, self.unit = sem, half, step, seed, before, unit
        self.layer = layer if layer is not None else B * half + FC * step

    def half_at(self, l, b, j):
        return l * (self.layer * self.unit) + b * (self.half * self.unit) + (self.seed + (self.before + j + 1) * self.unit)

    def step_at(self, l, c, j):
        at = self.before + B * self.half
        return l * (self.layer * self.unit) + c * (self.step * self.unit) + (self.seed + (at + j + 1) * self.unit)

    def layer_at(self, l, j):
        return l * (self.layer * self.unit) + (self.seed + (j + 1) * self.unit)


def encoder_trunk(nc, xT, watt, wffn, tables, gains, lam, out):
    with ExitStack() as ctx:
        KB = 1024
        cursor = [nc.sbuf_base + (-nc.sbuf_base) % 64]

        def region(size):
            at = cursor[0]
            cursor[0] += size
            return at

        def at(name, shape, offset, dt=F32):
            return nc.alloc_sbuf_tensor_at(name, shape, dt, offset=offset)

        def psum(name):
            return ctx.enter_context(nc.psum_tensor(name, [P, T], F32))

        r_x = region(32 * KB)
        r_h = region(32 * KB)
        r_yv = region(32 * KB)
        r_raw = region(RAW * 4 * KB)
        r_w = region(WS_ATT * 8 * KB)
        r_qk = region(24 * KB)
        r_at = region(16 * KB)
        r_e = region(8 * KB)
        r_ckv = region(4 * KB)
        r_s = region(16 * KB)
        r_c = region(4 * KB + 1024 + 256 * 5 )
        assert cursor[0] <= nc.sbuf_usable_end, (cursor[0], nc.sbuf_usable_end)

        x = at("x", [P, B, KT, T], r_x)
        h0 = [at(f"h0_{s}", [P, KT, T], r_h + i * 16 * KB, F32R) for i, s in enumerate(("hi", "lo"))]
        h1 = [at(f"h1_{s}", [P, KT, T], r_yv + i * 16 * KB, F32R) for i, s in enumerate(("hi", "lo"))]
        ydiff = [at(f"ydiff_{s}", [P, H, T], r_yv + i * 8 * KB, F32R) for i, s in enumerate(("hi", "lo"))]
        v = [at(f"v_{s}", [P, NT, H * P], r_yv + (16 + i * 8) * KB, F32R) for i, s in enumerate(("hi", "lo"))]
        raw = at("raw", [P, RAW, CH], r_raw)
        w = [[at(f"w_{s}{n}", [P, CH], r_w + (n * 8 + i * 4) * KB, F32R) for i, s in enumerate(("hi", "lo"))]
             for n in range(WS_FFN)]
        qd = [[[at(f"qd{n}{c}_{s}", [P, T], r_qk + (n * 12 + c * 4 + i * 2) * KB, F32R)
                for i, s in enumerate(("hi", "lo"))] for c in range(2)] for n in range(2)]
        kd = [[at(f"kd{n}_{s}", [P, T], r_qk + (n * 12 + 8 + i * 2) * KB, F32R)
               for i, s in enumerate(("hi", "lo"))] for n in range(2)]
        cq = [[at(f"cq{n}_{s}", [P, T], r_qk + (n * 4 + i * 2) * KB, F32R)
               for i, s in enumerate(("hi", "lo"))] for n in range(2)]
        kpe = [at(f"kpe_{s}", [P, T], r_qk + (8 + i * 2) * KB, F32R) for i, s in enumerate(("hi", "lo"))]
        ckv = [at(f"ckv_{s}", [P, T], r_ckv + i * 2 * KB, F32R) for i, s in enumerate(("hi", "lo"))]
        ymla = [[at(f"ymla{n}_{s}", [P, T], (r_qk + (12 + n * 4 + i * 2) * KB) if n < 3 else r_ckv + i * 2 * KB, F32R)
                 for i, s in enumerate(("hi", "lo"))] for n in range(H)]
        qpe = [at(f"qpe{n}", [P, T], r_h + n * 2 * KB, F32R) for n in range(H)]
        qn = [[at(f"qn{n}_{s}", [P, T], r_h + (16 + n * 4 + i * 2) * KB, F32R)
               for i, s in enumerate(("hi", "lo"))] for n in range(2)]
        kn = [[at(f"kn{n}_{s}", [P, T], r_h + (24 + n * 4 + i * 2) * KB, F32R)
               for i, s in enumerate(("hi", "lo"))] for n in range(2)]
        aT = [[at(f"aT{n}_{s}", [P, NT, 2 * P], r_at + (n * 8 + i * 4) * KB, F32R)
               for i, s in enumerate(("hi", "lo"))] for n in range(2)]
        u = [[[at(f"u{t}{b}_{s}", [P, T], r_at + (t * 8 + b * 4 + i * 2) * KB, F32R)
               for i, s in enumerate(("hi", "lo"))] for b in range(B)] for t in range(2)]
        h0_t = at("h0_t", [P, KT, T], r_h + 16 * KB)
        h1_t = at("h1_t", [P, KT, T], r_yv + 16 * KB)
        ydiff_t = at("ydiff_t", [P, H, T], r_yv + 8 * KB)
        cq_t = [at(f"cq_t{n}", [P, T], r_qk + (n * 4 + 2) * KB) for n in range(2)]
        ckv_t = at("ckv_t", [P, T], r_ckv + 2 * KB)
        e = [at(f"e{n}", [P, T], r_e + n * 2 * KB if n < 4 else r_s + n * 2 * KB) for n in range(6)]
        silu = [at(f"silu{n}", [P, T], r_e + n * 2 * KB) for n in range(2)]
        gated = [at(f"gated{n}", [P, T], r_e + (4 + n * 2) * KB) for n in range(2)]
        sq = [at(f"sq{n}", [P, T], r_s + n * 2 * KB) for n in range(2)]
        acc = at("acc", [P, T], r_s + 4 * KB)
        dg = at("dg", [P, NT, P], r_s + 6 * KB)
        r1 = at("r1", [P, T], r_s + 12 * KB)
        r2 = at("r2", [P, T], r_s + 14 * KB)
        cs = at("cs", [P, 2, T], r_c)
        small = [r_c + 4 * KB]

        def little(name, n, dt=F32):
            o = small[0]
            small[0] += -(-n * 4 // 32) * 32
            assert small[0] <= cursor[0], name
            return at(name, [P, n], o, dt)

        ident = little("ident", P)
        masks = little("masks", 4)
        ones = little("ones", P)
        g = little("g", 4 * L * KT + KT)
        gsmall = little("gsmall", L * 4)
        gsub = little("gsub", L)
        lamv = little("lamv", 2 * L)
        mx = little("mx", NEV)
        ls = little("ls", NEV)
        rc = little("rc", 4)
        ms = [little(f"ms{n}", NT) for n in range(3)]
        yi = little("yi", NT, I32)
        yy = little("yy", NT)
        zero = little("zero", 1)
        sq_out = at("sq_out", [P, KT, T], r_yv)
        acc_out = at("acc_out", [P, T], r_yv + 16 * KB)
        dg_out = at("dg_out", [P, NT, P], r_yv + 18 * KB)
        y_out = at("y_out", [P, B, KT, T], r_h)
        lamt = e[0]

        bank = [psum(f"bank{n}") for n in range(8)]
        tail = 7

        def sem(name):
            return ctx.enter_context(nc.semaphore(name))

        s_load = sem("constants_loaded")
        s_x0 = [sem(f"x0_loaded{n}") for n in range(KT // 2)]
        s_x1 = sem("x1_loaded")
        s_cs = sem("rope_tables_loaded")
        s_raw = [Count(sem(f"raw_loaded{n}"), half=NCH // RAW, step=FCH // RAW, seed=0, unit=16) for n in range(RAW)]
        s_hi = Count(sem("weights_hi"), NCH, FCH)
        s_lo = Count(sem("weights_lo"), NCH, FCH)
        s_mm = Count(sem("projection_done"), NMM, FMM)
        s_plain_hi = Count(sem("plain_hi"), len(PLAIN))
        s_plain_lo = Count(sem("plain_lo"), len(PLAIN))
        s_rope_read = Count(sem("rope_bank_read"), len(ROPED))
        s_roped = Count(sem("roped"), len(ROPED))
        s_rope_hi = Count(sem("rope_hi"), len(ROPE_SPLITS))
        s_rope_lo = Count(sem("rope_lo"), len(ROPE_SPLITS))
        s_latent = Count(sem("latent_copied"), len(LATENT))
        s_xo = Count(sem("output_added"), len(OUTS))
        s_score = Count(sem("scores_done"), NEV)
        s_max = Count(sem("max_done"), NEV)
        s_exp = Count(sem("exp_done"), NEV)
        s_prob = Count(sem("probs_done"), UNITS)
        s_tr = Count(sem("transposed"), UNITS)
        s_at_hi = Count(sem("aT_hi"), UNITS)
        s_at_lo = Count(sem("aT_lo"), UNITS)
        s_av = Count(sem("av_done"), UNITS // 2)
        s_oc = Count(sem("diff_out_copied"), H)
        s_ym_hi = Count(sem("latent_out_hi"), H)
        s_ym_lo = Count(sem("latent_out_lo"), H)
        s_sq = Count(sem("squares"), NSQ, layer=NSQ_LAYER, before=KT)
        s_add = Count(sem("squares_added"), NADD, layer=NADD_LAYER, before=KT)
        s_st = Count(sem("sums_done"), NSTAT, layer=NSTAT_LAYER, before=1)
        s_dg = Count(sem("rstd_diagonal"), NSTAT, layer=NSTAT_LAYER, before=1)
        s_rb = Count(sem("rstd_spread"), NSTAT, layer=NSTAT_LAYER, before=1)
        s_t = Count(sem("normed"), NSQ, layer=NSQ_LAYER, before=KT)
        s_t_hi = Count(sem("normed_hi"), NSQ, layer=NSQ_LAYER, before=KT)
        s_t_lo = Count(sem("normed_lo"), NSQ, layer=NSQ_LAYER, before=KT)
        s_silu = Count(sem("silu_done"), 0, 4)
        s_gated = Count(sem("gated"), 0, 4)
        s_u_hi = Count(sem("u_hi"), 0, 4)
        s_u_lo = Count(sem("u_lo"), 0, 4)
        s_xf = Count(sem("ffn_added"), 0, 2 * KT)
        LINKS_HALF = NSTAT * RSQRT_LINKS + 3 * 16 + 16
        s_link = Count(sem("vector_chain"), LINKS_HALF, layer=B * LINKS_HALF + 2 * RSQRT_LINKS, before=RSQRT_LINKS)
        s_final = sem("vector_final")
        s_act = sem("scalar_final")
        s_pe = sem("tensor_final")
        s_pre = sem("vector_setup")
        s_prea = sem("scalar_setup")
        s_out = sem("out_stored")

        def norm_counts(which, l, b=0):
            if which == "first":
                return (lambda c, j: c.layer_at(l, j)), 0, 0, 0
            if which == "next":
                return (lambda c, j: c.layer_at(l, c.layer + j)), 0, 0, 0
            if which == "last":
                return (lambda c, j: c.layer_at(l, j)), KT + B * NSQ, KT + B * NADD, 1 + B * NSTAT
            return (lambda c, j: c.half_at(l, b, j)), SQUARES["n"][0], 0, STATS.index("n")

        def product(pe, out_ap, lhs, rhs, first, last):
            nc.tensor.matmul(out_ap, lhs[0], rhs[0], start=first, stop=False)
            nc.tensor.matmul(out_ap, lhs[0], rhs[1], start=False, stop=False)
            return nc.tensor.matmul(out_ap, lhs[1], rhs[0], start=False, stop=last)

        def stacked_product(pe, out_ap, lhs, rhs, first):
            nc.tensor.matmul(out_ap, lhs, rhs[0], start=first, stop=False)
            return nc.tensor.matmul(out_ap, lhs, rhs[1], start=False, stop=True)

        def rope_target(name):
            if name == "kpe":
                return [kpe], None
            n = int(name[-1])
            if name[0] == "p":
                return [qpe[2 * n], qpe[2 * n + 1]], 2
            return (qd[n % 2], 0) if name[0] == "q" else ([kd[n % 2]], None)

        def plain_target(name):
            n = int(name[2])
            if name[:2] == "vm":
                return [v[s][:, n, :] for s in range(2)]
            return [(qn if name[0] == "q" else kn)[n % 2][s][:] for s in range(2)]

        def normed_target(name, q):
            if name[0] == "y":
                n = int(name[1])
                return [ydiff[s][:, n, :] for s in range(2)], ydiff_t[:, n, :]
            if name == "ckv":
                return [ckv[s][:] for s in range(2)], ckv_t[:]
            return [cq[q][s][:] for s in range(2)], cq_t[q][:]

        block = ctx.enter_context(nc.Block())

        @block.sync
        def _(sp):
            sp.dma_start(ident[:], tables[:, 2 * T:2 * T + P]).then_inc(s_load, 16)
            sp.dma_start(masks[:], tables[:, 2 * T + P:2 * T + P + 4]).then_inc(s_load, 16)
            sp.dma_start(g[:], gains[:, 0:g.shape[1]]).then_inc(s_load, 16)
            sp.dma_start(gsmall[:], gains[:, g.shape[1]:]).then_inc(s_load, 16)
            sp.dma_start(lamt[:], lam).then_inc(s_load, 16)
            for k in range(0, KT, 2):
                sp.dma_start(x[:, 0, k:k + 2, :], xT[0, :, k:k + 2, :]).then_inc(s_x0[k // 2], 16)
            with sp.Fori(0, L) as l:
                with sp.Fori(0, B) as b:
                    for j in range(NCH):
                        sp.wait_ge(s_lo.sem, s_lo.half_at(l, b, j - RAW))
                        sp.dma_start(raw[:, j % RAW, :], watt[bass.ds(l * NCH + j, 1), :, :].rearrange(
                            "o p n -> p (o n)")).then_inc(s_raw[j % RAW].sem, 16)
                with sp.Fori(0, FC) as c:
                    for j in range(FCH):
                        sp.wait_ge(s_lo.sem, s_lo.step_at(l, c, j - RAW))
                        sp.dma_start(raw[:, j % RAW, :], wffn[bass.ds(l * (FC * FCH) + c * FCH + j, 1), :, :].rearrange(
                            "o p n -> p (o n)")).then_inc(s_raw[j % RAW].sem, 16)
            for n in range(B * KT):
                sp.wait_ge(s_final, FINAL_T[n])
                sp.dma_start(out[n // KT, :, n % KT, :], y_out[:, n // KT, n % KT, :]).then_inc(s_out, 16)
            sp.wait_ge(s_out, 16 * B * KT)

        @block.gpsimd
        def _(pool):
            pool.memset(ones[:], 1.0).then_inc(s_pre, 1)
            for c in (s_hi, s_lo, s_add):
                pool.sem_inc(c.sem, SEED)

            def split(j, slot, raw_at, hi_at):
                src = raw[:, j % RAW, :]
                pool.wait_ge(s_raw[j % RAW].sem, raw_at)
                nc.gpsimd.tensor_tensor(w[slot][0][:], src, zeros_like(src), ALU.add).then_inc(s_hi.sem, 1)
                pool.wait_ge(s_hi.sem, hi_at)
                nc.gpsimd.tensor_tensor(w[slot][1][:], src, w[slot][0][:].bitcast(F32), ALU.subtract).then_inc(s_lo.sem, 1)

            pool.memset(zero[:], 0.0).then_inc(s_pre, 1)
            pool.wait_ge(s_pre, 2)

            def zeros_like(src):
                return zero[:].to_broadcast([P, CH])

            def add_squares(which, l, b=0):
                f, sq0, add0, st0 = norm_counts(which, l, b)
                sq_at = SQUARED[("n", 0)] if which == "tail" else sq0
                for k in range(KT):
                    pool.wait_ge(s_sq.sem, f(s_sq, sq_at + k))
                    if k == 0:
                        pool.wait_ge(s_st.sem, f(s_st, st0 - 1))
                        nc.gpsimd.tensor_tensor(acc[:], sq[0][:], zero[:].to_broadcast([P, T]), ALU.add).then_inc(s_add.sem, 1)
                    else:
                        pool.wait_ge(s_add.sem, f(s_add, add0 + k - 1))
                        nc.gpsimd.tensor_tensor(acc[:], acc[:], sq[k % 2][:], ALU.add).then_inc(s_add.sem, 1)

            def ffn_split(l, c, j):
                split(j, j, s_raw[j % RAW].step_at(l, c, j // RAW), s_hi.step_at(l, c, j))

            add_squares("first", 0)
            with pool.Fori(0, L) as l:
                with pool.Fori(0, B) as b:
                    for j in range(NCH):
                        if j < WS_ATT:
                            ffn_free = FCHUNK_FREE[j] - FMM
                            half_free = CHUNK_FREE[j - WS_ATT] - NMM
                            pool.wait_ge(s_mm.sem, s_mm.half_at(l, b, ffn_free) + b * (half_free - ffn_free))
                        else:
                            pool.wait_ge(s_mm.sem, s_mm.half_at(l, b, CHUNK_FREE[j - WS_ATT]))
                        split(j, j % WS_ATT, s_raw[j % RAW].half_at(l, b, j // RAW), s_hi.half_at(l, b, j))
                        if CHUNKS[j] == "oa0":
                            add_squares("tail", l, b)
                for j in range(FCH):
                    pool.wait_ge(s_mm.sem, s_mm.half_at(l, 1, CHUNK_FREE[NCH - WS_ATT + j] if j < WS_ATT else NMM - 1))
                    ffn_split(l, 0, j)
                with pool.Fori(1, FC) as c:
                    for j in range(FCH):
                        pool.wait_ge(s_mm.sem, s_mm.step_at(l, c, FCHUNK_FREE[j] - FMM))
                        ffn_split(l, c, j)
                add_squares("next", l)

        @block.tensor
        def _(pe):
            for c in (s_mm, s_score, s_tr, s_av, s_st, s_rb):
                pe.sem_inc(c.sem, SEED)

            def sums(wait, free, terms):
                pe.wait_ge(*wait)
                pe.wait_ge(*free)
                for m in range(NT):
                    for n, term in enumerate(terms):
                        last = nc.tensor.matmul(bank[tail][:, m:m + 1], term[:, m * P:(m + 1) * P], ones[:, 0:1],
                                                start=n == 0, stop=n == len(terms) - 1)
                last.then_inc(s_st.sem, 1)

            def spread(wait, done):
                pe.wait_ge(*wait)
                nc.tensor.matmul(bank[tail][:], ones[:], dg[:].rearrange("p m t -> p (m t)"), start=True,
                                 stop=True).then_inc(done, 1)

            def norm_sums(which, l, b=0):
                f, sq0, add0, st0 = norm_counts(which, l, b)
                sums((s_add.sem, f(s_add, add0 + KT - 1)), (s_t.sem, f(s_t, sq0 - 1)), [acc])

            def norm_spread(which, l, b=0):
                f, sq0, add0, st0 = norm_counts(which, l, b)
                spread((s_dg.sem, f(s_dg, st0)), s_rb.sem)

            def chunk(l, b, j):
                pe.wait_ge(s_lo.sem, s_lo.half_at(l, b, j))
                return w[j % WS_ATT]

            def bank_read(l, b, i):
                name = TILES[i] if i >= 0 else TILES[NTILE + i]
                back = 0 if i >= 0 else 1
                for table, count in ((ROPED, s_rope_read), (PLAIN, s_plain_lo), (LATENT, s_latent), (OUTS, s_xo)):
                    if name in table:
                        pe.wait_ge(count.sem, count.half_at(l, b, table[name] - back * len(table)))

            def project(l, b, name, halves):
                i = TILE[name]
                dst = bank[i % 2][:]
                wc = chunk(l, b, chunk_of(name))
                if name[0] in "qk" and name[1].isdigit() or name in ("ckv", "kpe", "cq0", "cq1"):
                    ops = [([wc[s][:, k * P:(k + 1) * P] for s in range(2)], [h0[s][:, k, :] for s in range(2)])
                           for k in range(KT)]
                elif name[:2] == "pe":
                    n = int(name[2])
                    pe.wait_ge(s_t_lo.sem, s_t_lo.half_at(l, b, SQUARES["cq"][1]))
                    ops = [([wc[s][:, k * 2 * P + n * P:k * 2 * P + (n + 1) * P] for s in range(2)],
                            [cq[k][s][:] for s in range(2)]) for k in range(2)]
                elif name[:2] == "qn":
                    n = int(name[2])
                    pe.wait_ge(s_t_lo.sem, s_t_lo.half_at(l, b, SQUARES["cq"][1]))
                    ops = [([wc[s][:, k * 4 * P + n * P:k * 4 * P + (n + 1) * P] for s in range(2)],
                            [cq[k][s][:] for s in range(2)]) for k in range(2)]
                elif name[:2] == "kn":
                    n = int(name[2])
                    pe.wait_ge(s_t_lo.sem, s_t_lo.half_at(l, b, SQUARES["ckv"][0]))
                    ops = [([wc[s][:, n * P:(n + 1) * P] for s in range(2)], [ckv[s][:] for s in range(2)])]
                elif name[:2] == "vm":
                    n = int(name[2])
                    ops = [([ckv[s][:, n * P:(n + 1) * P] for s in range(2)], [wc[s][:, 4 * P:8 * P] for s in range(2)])]
                else:
                    n = int(name[2])
                    y = [[ydiff[s][:, k, :] for s in range(2)] for k in range(H)] if name[1] == "a" else \
                        [[ymla[k][s][:] for s in range(2)] for k in range(H)]
                    ops = [([wc[s][:, k * 2 * P + (n % 2) * P:k * 2 * P + (n % 2 + 1) * P] for s in range(2)], y[k])
                           for k in range(H)]
                    if name[1] == "a":
                        pe.wait_ge(s_t_lo.sem, s_t_lo.half_at(l, b, SQUARES["y3"][0]))
                lo, hi = {"all": (0, len(ops)), "a": (0, len(ops) // 2), "b": (len(ops) // 2, len(ops))}[halves]
                if lo == 0:
                    bank_read(l, b, i - 2)
                for n in range(lo, hi):
                    if name in ("ob0", "ob1") and n == H - 1:
                        pe.wait_ge(s_ym_lo.sem, s_ym_lo.half_at(l, b, H - 1))
                    last = product(pe, dst, ops[n][0], ops[n][1], n == 0, n == len(ops) - 1)
                if hi == len(ops):
                    last.then_inc(s_mm.sem, 1)

            def values(l, b):
                for j in range(4):
                    wc = chunk(l, b, j)
                    if j == 0:
                        pe.wait_ge(s_exp.sem, s_exp.half_at(l, b, -1))
                        pe.wait_ge(s_at_lo.sem, s_at_lo.half_at(l, b, -1))
                    pe.wait_ge(s_t_lo.sem, s_t_lo.half_at(l, b, 2 * j + 1 - KT))
                    for m in range(NT):
                        for kk in range(2):
                            k = 2 * j + kk
                            last = product(pe, bank[2 + m][:], [h0[s][:, k, m * P:(m + 1) * P] for s in range(2)],
                                           [wc[s][:, kk * 4 * P:(kk + 1) * 4 * P] for s in range(2)], k == 0, k == KT - 1)
                        if j == 3 or m == NT - 1:
                            last.then_inc(s_mm.sem, 1)

            def scores(l, b, i):
                h, qt = i // NT, i % NT
                at_q = slice(qt * P, (qt + 1) * P)
                for c in range(2 if i < 16 else 1):
                    ev = 2 * i + c if i < 16 else 32 + i - 16
                    dst = bank[2 + ev % 3][:]
                    pe.wait_ge(s_exp.sem, s_exp.half_at(l, b, ev - 3))
                    if ev < 3:
                        pe.wait_ge(s_plain_lo.sem, s_plain_lo.half_at(l, b, PLAIN[f"dv{ev}"]))
                    if i < 16:
                        if qt == 0:
                            pe.wait_ge(s_rope_lo.sem, s_rope_lo.half_at(l, b, ROPE_SPLITS[(f"k{h}", 0)]))
                        last = product(pe, dst, [qd[h % 2][c][s][:, at_q] for s in range(2)],
                                       [kd[h % 2][s][:] for s in range(2)], True, True)
                    else:
                        h -= H
                        if qt == 0:
                            pe.wait_ge(s_plain_lo.sem, s_plain_lo.half_at(l, b, PLAIN[f"qn{h}"]))
                            pe.wait_ge(s_rope_lo.sem, s_rope_lo.half_at(l, b, ROPE_SPLITS[(f"pe{h // 2}", h % 2)]))
                        product(pe, dst, [qn[h % 2][s][:, at_q] for s in range(2)], [kn[h % 2][s][:] for s in range(2)],
                                True, False)
                        last = stacked_product(pe, dst, qpe[h][:, at_q], [kpe[s][:] for s in range(2)], False)
                    last.then_inc(s_score.sem, 1)

            def transposes(l, b, i):
                src = e[e_buffer(2 * i if i < 16 else 16 + i)]
                pe.wait_ge(s_prob.sem, s_prob.half_at(l, b, i))
                pe.wait_ge(s_at_lo.sem, s_at_lo.half_at(l, b, i - 1))
                if i == 0:
                    pe.wait_ge(s_plain_lo.sem, s_plain_lo.half_at(l, b, PLAIN["dv3"]))
                for k in range(NT):
                    last = nc.tensor.transpose(bank[5][:, k * P:(k + 1) * P], src[:, k * P:(k + 1) * P], ident[:])
                last.then_inc(s_tr.sem, 1)

            def apply_values(l, b, a):
                h, half = a // 2, a % 2
                pe.wait_ge(s_at_lo.sem, s_at_lo.half_at(l, b, 2 * a + 1))
                if half == 0:
                    if h == 0:
                        pe.wait_ge(s_ym_lo.sem, s_ym_lo.half_at(l, b, -1))
                    elif h <= H:
                        pe.wait_ge(s_oc.sem, s_oc.half_at(l, b, h - 1))
                    else:
                        pe.wait_ge(s_ym_lo.sem, s_ym_lo.half_at(l, b, h - H - 1))
                if a == 8:
                    pe.wait_ge(s_plain_lo.sem, s_plain_lo.half_at(l, b, PLAIN["vm3"]))
                dst = bank[6][:, half * 2 * P:(half + 1) * 2 * P]
                for k in range(NT):
                    last = product(pe, dst, [v[s][:, k, (h % H) * P:(h % H + 1) * P] for s in range(2)],
                                   [aT[a % 2][s][:, k, :] for s in range(2)], k == 0, k == NT - 1)
                last.then_inc(s_av.sem, 1)

            def ffn_step(l, c, first):
                for tt in range(2):
                    for b in range(B):
                        ev = 2 * tt + b
                        hb = h0 if b == 0 else h1
                        for part in range(2):
                            dst = bank[2 * part + ev % 2][:]
                            j = 2 * tt + part
                            pe.wait_ge(s_lo.sem, s_lo.step_at(l, c, j))
                            if not first or ev >= 2:
                                last_read = s_silu if part == 0 else s_gated
                                pe.wait_ge(last_read.sem, last_read.step_at(l, c, ev - 2))
                            elif part == 0:
                                pe.wait_ge(s_xo.sem, s_xo.half_at(l, 1, len(OUTS) - 1))
                            else:
                                pe.wait_ge(s_exp.sem, s_exp.half_at(l, 1, NEV - 1))
                            if first and tt == 0:
                                if b == 0:
                                    pe.wait_ge(s_t_lo.sem, s_t_lo.half_at(l, 1, NSQ - 1))
                                elif part == 0:
                                    norm_spread("last", l)
                            for k in range(KT):
                                if first and ev == 1 and part == 0:
                                    pe.wait_ge(s_t_lo.sem, s_t_lo.layer_at(l, NSQ_LAYER - KT + k))
                                last = product(pe, dst, [w[j][s][:, k * P:(k + 1) * P] for s in range(2)],
                                               [hb[s][:, k, :] for s in range(2)], k == 0, k == KT - 1)
                            last.then_inc(s_mm.sem, 1)
                            if first and ev == 0 and part == 0:
                                norm_sums("last", l)
                for b in range(B):
                    for n in range(KT):
                        ev = b * KT + n
                        if n == 0:
                            pe.wait_ge(s_u_lo.sem, s_u_lo.step_at(l, c, 2 + b))
                            if b == 0:
                                pe.wait_ge(s_lo.sem, s_lo.step_at(l, c, 5))
                        if not first or ev >= 4:
                            pe.wait_ge(s_xf.sem, s_xf.step_at(l, c, ev - 4))
                        elif ev == 0:
                            pe.wait_ge(s_t.sem, s_t.layer_at(l, NSQ_LAYER - 1))
                            pe.wait_ge(s_ym_lo.sem, s_ym_lo.half_at(l, 1, H - 1))
                            pe.wait_ge(s_at_lo.sem, s_at_lo.half_at(l, 1, UNITS - 1))
                        for tt in range(2):
                            last = product(pe, bank[4 + ev % 4][:], [w[4 + tt][s][:, n * P:(n + 1) * P] for s in range(2)],
                                           [u[tt][b][s][:] for s in range(2)], tt == 0, tt == 1)
                        last.then_inc(s_mm.sem, 1)

            pe.wait_ge(s_load, 5 * 16)
            pe.wait_ge(s_pre, PRE_DVE)
            norm_sums("first", 0)
            norm_spread("first", 0)
            with pe.Fori(0, L) as l:
                with pe.Fori(0, B) as b:
                    for step in TENSOR_ORDER:
                        kind = step[0]
                        if kind == "V":
                            values(l, b)
                        elif kind in ("P", "Pa", "Pb"):
                            project(l, b, step[1], {"P": "all", "Pa": "a", "Pb": "b"}[kind])
                        elif kind == "S":
                            scores(l, b, step[1])
                        elif kind == "T":
                            transposes(l, b, step[1])
                        elif kind == "A":
                            apply_values(l, b, step[1])
                        elif kind == "ST":
                            name = step[1]
                            if name == "n":
                                wait = (s_add.sem, s_add.half_at(l, b, KT - 1))
                            else:
                                wait = (s_sq.sem, s_sq.half_at(l, b, SQUARED[(name, len(SQUARES[name]) - 1)]))
                            sums(wait, (s_t.sem, s_t.half_at(l, b, SQUARES[name][0] - 1)), sq if name == "cq" else [acc])
                        elif kind == "RB":
                            spread((s_dg.sem, s_dg.half_at(l, b, STATS.index(step[1]))), s_rb.sem)
                ffn_step(l, 0, True)
                with pe.Fori(1, FC) as c:
                    ffn_step(l, c, False)
                pe.wait_ge(s_xf.sem, s_xf.layer_at(l, s_xf.layer - 1))
                norm_sums("next", l)
                norm_spread("next", l)
            pe.wait_ge(s_final, FINAL_ADD)
            for m in range(NT):
                last = nc.tensor.matmul(bank[6][:, m:m + 1], acc_out[:, m * P:(m + 1) * P], ones[:, 0:1], start=True, stop=True)
            last.then_inc(s_pe, 1)
            pe.wait_ge(s_final, FINAL_DG)
            nc.tensor.matmul(bank[6][:], ones[:], dg_out[:].rearrange("p m t -> p (m t)"), start=True, stop=True).then_inc(s_pe, 1)

        @block.scalar
        def _(act):
            for c in (s_plain_hi, s_rope_hi, s_latent, s_exp, s_at_hi, s_oc, s_ym_hi, s_sq, s_t_hi, s_silu, s_u_hi):
                act.sem_inc(c.sem, SEED)
            act.wait_ge(s_load, 5 * 16)
            act.wait_ge(s_pre, PRE_LAM)
            nc.scalar.activation(rc[:, 0:2 * L], lamv[:, 0:2 * L], ACT.Exp).then_inc(s_prea, 1)

            def norm_square(which, l, b, k):
                f, sq0, add0, st0 = norm_counts(which, l, b)
                if which == "first" and k % 2 == 0:
                    act.wait_ge(s_x0[k // 2], 16)
                if k == 0:
                    if which == "next":
                        act.wait_ge(s_xf.sem, s_xf.layer_at(l, s_xf.layer - 1 - KT))
                    elif which == "tail":
                        act.wait_ge(s_xf.sem, s_xf.layer_at(l, -1))
                        act.wait_ge(s_xo.sem, s_xo.half_at(l, b, -1))
                if which == "last":
                    act.wait_ge(s_xo.sem, s_xo.half_at(l, 1, OUTS[f"ob{k}"]))
                if k < 2:
                    act.wait_ge(s_st.sem, f(s_st, st0 - 1))
                else:
                    act.wait_ge(s_add.sem, f(s_add, add0 + k - 2))
                src = {"first": x[:, 0, k, :], "next": x[:, 0, k, :], "last": x[:, 1, k, :]}.get(which)
                if src is None:
                    src = x[:, bass.ds(b * -1 + 1, 1), k, :].rearrange("p o t -> p (o t)")
                nc.scalar.activation(sq[k % 2][:], src, ACT.Square).then_inc(s_sq.sem, 1)

            def norm_hi(which, l, b, k):
                f, sq0, add0, st0 = norm_counts(which, l, b)
                hi, full = (h1[0], h1_t) if which == "last" else (h0[0], h0_t)
                act.wait_ge(s_t.sem, f(s_t, sq0 + k))
                nc.scalar.activation(hi[:, k, :], full[:, k, :], ACT.Copy).then_inc(s_t_hi.sem, 1)

            def rope_his(l, b, name):
                dst, scale = rope_target(name)
                act.wait_ge(s_roped.sem, s_roped.half_at(l, b, ROPED[name]))
                for c, d in enumerate(dst):
                    nc.scalar.activation((d if name[0] == "p" else d[0])[:], r1[:], ACT.Copy, scale=1.0 if scale is None else
                                         masks[:, scale + c:scale + c + 1]).then_inc(s_rope_hi.sem, 1)

            def latent_copy(l, b, name):
                i = TILE[name]
                src = bank[i % 2][:]
                n = int(name[2]) if name[1] == "q" else 0
                stat = "cq" if name[1] == "q" else "ckv"
                act.wait_ge(s_mm.sem, s_mm.half_at(l, b, DV_MM + i))
                act.wait_ge(s_st.sem, s_st.half_at(l, b, STATS.index("ckv") - 1))
                nc.scalar.activation((acc if stat == "ckv" else sq[n])[:], src, ACT.Square).then_inc(s_sq.sem, 1)
                nc.scalar.activation(normed_target(stat, n)[1], src, ACT.Copy).then_inc(s_latent.sem, 1)

            def plain_hi(l, b, name):
                i = TILE[name]
                act.wait_ge(s_mm.sem, s_mm.half_at(l, b, DV_MM + i))
                nc.scalar.activation(plain_target(name)[0], bank[i % 2][:], ACT.Copy,
                                     scale=MLA_SCALE if name[:2] == "qn" else 1.0).then_inc(s_plain_hi.sem, 1)

            def exponentials(l, b, i):
                for ev in ([2 * i, 2 * i + 1] if i < 16 else [16 + i]):
                    act.wait_ge(s_max.sem, s_max.half_at(l, b, ev))
                    act.wait_ge(s_tr.sem, s_tr.half_at(l, b, e_before(ev)))
                    nc.scalar.activation(e[e_buffer(ev)][:], bank[2 + ev % 3][:], ACT.Exp, bias=mx[:, ev:ev + 1],
                                         accum_out=ls[:, ev:ev + 1]).then_inc(s_exp.sem, 1)

            def transposed_hi(l, b, i):
                act.wait_ge(s_tr.sem, s_tr.half_at(l, b, i))
                act.wait_ge(s_av.sem, s_av.half_at(l, b, i // 2 - 2))
                dst = aT[i // 2 % 2][0][:, :, (i % 2) * P:(i % 2 + 1) * P]
                nc.scalar.activation(dst, bank[5][:].rearrange("p (k q) -> p k q", k=NT), ACT.Copy).then_inc(s_at_hi.sem, 1)

            def head_out(l, b, h):
                act.wait_ge(s_av.sem, s_av.half_at(l, b, 2 * h + 1))
                if h < H:
                    act.wait_ge(s_st.sem, s_st.half_at(l, b, STATS.index({2: "ckv", 3: "y2"}.get(h, f"y{h}")) - (h < 2)))
                    nc.scalar.activation(acc[:], bank[6][:], ACT.Square).then_inc(s_sq.sem, 1)
                    nc.scalar.activation(normed_target(f"y{h}", 0)[1], bank[6][:], ACT.Copy,
                                         scale=gsub[:, bass.ds(l, 1)]).then_inc(s_oc.sem, 1)
                else:
                    nc.scalar.activation(ymla[h - H][0][:], bank[6][:], ACT.Copy).then_inc(s_ym_hi.sem, 1)

            def normed_hi(l, b, name):
                for q, n in enumerate(SQUARES[name]):
                    act.wait_ge(s_t.sem, s_t.half_at(l, b, n))
                    dst, src = normed_target(name, q)
                    nc.scalar.activation(dst[0], src, ACT.Copy).then_inc(s_t_hi.sem, 1)

            for k in range(KT):
                norm_square("first", 0, 0, k)
                if k == KT - 2:
                    act.dma_start(cs[:], tables[:, 0:2 * T].rearrange("p (a t) -> p a t", a=2)).then_inc(s_cs, 16)
                    for kk in (0, KT // 2):
                        act.dma_start(x[:, 1, kk:kk + KT // 2, :], xT[1, :, kk:kk + KT // 2, :]).then_inc(s_x1, 16)
            with act.Fori(0, L) as l:
                for k in range(KT):
                    norm_hi("first", l, 0, k)
                act.wait_ge(s_x1, 2 * 16)
                with act.Fori(0, B) as b:
                    for step in SCALAR_ORDER:
                        kind, what = step[0], step[-1]
                        if kind == "V":
                            for m in range(NT):
                                act.wait_ge(s_mm.sem, s_mm.half_at(l, b, 3 + m))
                                nc.scalar.activation(v[0][:, m, :], bank[2 + m][:], ACT.Copy).then_inc(s_plain_hi.sem, 1)
                        elif kind == "RH":
                            rope_his(l, b, what)
                        elif kind == "LC":
                            latent_copy(l, b, what)
                        elif kind == "PH":
                            plain_hi(l, b, what)
                        elif kind == "EX":
                            exponentials(l, b, what)
                        elif kind == "TH":
                            transposed_hi(l, b, what)
                        elif kind == "YC":
                            head_out(l, b, what)
                        elif kind == "SH":
                            normed_hi(l, b, what)
                        elif kind == "SQ":
                            norm_square("tail", l, b, what)
                        elif kind == "SN":
                            norm_hi("tail", l, b, what)
                for k in range(KT):
                    norm_square("last", l, 0, k)
                for k in range(KT):
                    norm_hi("last", l, 0, k)
                with act.Fori(0, FC) as c:
                    for ev in range(4):
                        tt, b = ev // 2, ev % 2
                        act.wait_ge(s_mm.sem, s_mm.step_at(l, c, 2 * ev))
                        act.wait_ge(s_gated.sem, s_gated.step_at(l, c, ev - 2))
                        if ev == 0:
                            act.wait_ge(s_tr.sem, s_tr.half_at(l, 1, UNITS - 1))
                        nc.scalar.activation(silu[ev % 2][:], bank[ev % 2][:], ACT.Silu).then_inc(s_silu.sem, 1)
                        act.wait_ge(s_gated.sem, s_gated.step_at(l, c, ev))
                        nc.scalar.activation(u[tt][b][0][:], gated[ev % 2][:], ACT.Copy).then_inc(s_u_hi.sem, 1)
                for k in range(KT):
                    norm_square("next", l, 0, k)
            act.wait_ge(s_xf.sem, s_xf.layer_at(L, -1))
            for k in range(KT):
                nc.scalar.activation(sq_out[:, k, :], x[:, 1, k, :], ACT.Square).then_inc(s_act, 1)

        @block.vector
        def _(dve):
            for c in (s_plain_lo, s_rope_read, s_roped, s_rope_lo, s_xo, s_max, s_prob, s_at_lo, s_ym_lo, s_dg, s_t,
                      s_t_lo, s_gated, s_u_lo, s_xf, s_link):
                dve.sem_inc(c.sem, SEED)
            pre = [2]

            def setup(ins):
                pre[0] += 1
                ins.then_inc(s_pre, 1)
                dve.wait_ge(s_pre, pre[0])

            dve.wait_ge(s_load, 5 * 16)
            dve.wait_ge(s_pre, 2)
            setup(nc.vector.tensor_tensor(e[1][:, 0:4 * DH], lamt[:, 0:4 * DH], lamt[:, 4 * DH:8 * DH], ALU.mult))
            setup(nc.vector.tensor_reduce(lamv[:], e[1][:, 0:4 * DH].rearrange("p (a d) -> p a d", a=4), AX_X, ALU.add))
            assert pre[0] == PRE_LAM
            dve.wait_ge(s_prea, 1)
            for l in range(L):
                setup(nc.vector.tensor_tensor(lamv[:, 2 * l + 1:2 * l + 2], rc[:, 2 * l + 1:2 * l + 2], rc[:, 2 * l:2 * l + 1],
                                              ALU.subtract))
                setup(nc.vector.tensor_scalar(lamv[:, 2 * l + 1:2 * l + 2], lamv[:, 2 * l + 1:2 * l + 2], -LAM_INIT[l], None,
                                              ALU.add))
                setup(nc.vector.memset(lamv[:, 2 * l:2 * l + 1], 1.0))
                setup(nc.vector.tensor_scalar(gsub[:, l:l + 1], gsmall[:, 4 * l:4 * l + 1], 1.0 - LAM_INIT[l], None, ALU.mult))
            assert pre[0] == PRE_DVE

            def rsqrt_diagonal(link, width, src, wait, done, dg=dg):
                dve.wait_ge(*wait)
                var = ms[0][:]
                a = ms[1][:]
                link(nc.vector.tensor_scalar(var, src, 1.0 / width, EPS, ALU.mult, ALU.add))
                link(nc.vector.tensor_scalar(yi[:], var.bitcast(I32), 1, None, ALU.logical_shift_right))
                link(nc.vector.tensor_scalar(yy[:].bitcast(I32), yi[:], -1.0, float(0x5F3759DF), ALU.mult, ALU.add))
                for _ in range(3):
                    link(nc.vector.tensor_tensor(a, yy[:], yy[:], ALU.mult))
                    link(nc.vector.scalar_tensor_tensor(a, a, -0.5, var, ALU.mult, ALU.mult))
                    link(nc.vector.scalar_tensor_tensor(yy[:], a, 1.5, yy[:], ALU.add, ALU.mult))
                nc.vector.tensor_tensor(dg[:], ident[:].unsqueeze(1).to_broadcast([P, NT, P]),
                                        yy[:].unsqueeze(2).to_broadcast([P, NT, P]), ALU.mult).then_inc(done, 1)

            def chain(value):
                n = [0]

                def link(ins):
                    ins.then_inc(s_link.sem, 1)
                    dve.wait_ge(s_link.sem, value(n[0]))
                    n[0] += 1
                return link, n

            def norm_rsqrt(which, l, b, link):
                f, sq0, add0, st0 = norm_counts(which, l, b)
                dve.wait_ge(s_rb.sem, f(s_rb, st0 - 1))
                rsqrt_diagonal(link, D, bank[tail][:, 0:NT], (s_st.sem, f(s_st, st0)), s_dg.sem)

            def norm_apply(which, l, b, k):
                f, sq0, add0, st0 = norm_counts(which, l, b)
                if k == 0:
                    dve.wait_ge(s_rb.sem, f(s_rb, st0))
                    if which == "tail":
                        dve.wait_ge(s_x1, 2 * 16)
                        dve.wait_ge(s_score.sem, s_score.half_at(l, b, NEV - 1))
                    if which == "last":
                        dve.wait_ge(s_mm.sem, s_mm.half_at(l, 1, NMM - 1))
                if which == "tail":
                    xk = x[:, bass.ds(b * -1 + 1, 1), k, :].rearrange("p o t -> p (o t)")
                    gk = g[:, bass.ds(l * (4 * KT) + b * KT + (KT + k), 1)]
                else:
                    n = 0 if which == "first" else 3
                    xk = x[:, 0 if which == "first" else 1, k, :]
                    gk = g[:, bass.ds(l * (4 * KT) + n * KT + k, 1)]
                dst = h1_t if which == "last" else h0_t
                nc.vector.scalar_tensor_tensor(dst[:, k, :], xk, gk, bank[tail][:], ALU.mult, ALU.mult).then_inc(s_t.sem, 1)

            def norm_lo(which, l, b, k):
                f, sq0, add0, st0 = norm_counts(which, l, b)
                hi, lo, full = (*h1, h1_t) if which == "last" else (*h0, h0_t)
                dve.wait_ge(s_t_hi.sem, f(s_t_hi, sq0 + k))
                nc.vector.tensor_tensor(lo[:, k, :], full[:, k, :], hi[:, k, :].bitcast(F32), ALU.subtract).then_inc(s_t_lo.sem, 1)

            def last_add(l, k):
                f, sq0, add0, st0 = norm_counts("last", l)
                dve.wait_ge(s_sq.sem, f(s_sq, sq0 + k))
                if k == 0:
                    dve.wait_ge(s_st.sem, f(s_st, st0 - 1))
                    nc.vector.tensor_copy(acc[:], sq[0][:]).then_inc(s_add.sem, 1)
                else:
                    dve.wait_ge(s_add.sem, f(s_add, add0 + k - 1))
                    nc.vector.tensor_tensor(acc[:], acc[:], sq[k % 2][:], ALU.add).then_inc(s_add.sem, 1)

            def norm_halves(which, l):
                for k in range(KT + 1):
                    if k < KT:
                        norm_apply(which, l, 0, k)
                    if k:
                        norm_lo(which, l, 0, k - 1)

            def rope(l, b, name):
                i = TILE[name]
                z = bank[i % 2]
                dve.wait_ge(s_mm.sem, s_mm.half_at(l, b, DV_MM + i))
                q0 = min(n for (tn, c), n in ROPE_SPLITS.items() if tn == name)
                dve.wait_ge(s_rope_lo.sem, s_rope_lo.half_at(l, b, q0 - 1))
                nc.vector.tensor_tensor(r1[:], z[:], cs[:, 0, :], ALU.mult)
                nc.vector.tensor_tensor(r2[0:64, :], z[64:128, :], cs[64:128, 1, :], ALU.mult)
                nc.vector.tensor_tensor(r2[64:128, :], z[0:64, :], cs[0:64, 1, :], ALU.mult).then_inc(s_rope_read.sem, 1)
                dve.wait_ge(s_rope_read.sem, s_rope_read.half_at(l, b, ROPED[name]))
                nc.vector.tensor_tensor(r1[:], r1[:], r2[:], ALU.add).then_inc(s_roped.sem, 1)

            def rope_los(l, b, name):
                q0 = min(n for (tn, c), n in ROPE_SPLITS.items() if tn == name)
                dst, scale = rope_target(name)
                for c, d in enumerate(dst):
                    dve.wait_ge(s_rope_hi.sem, s_rope_hi.half_at(l, b, q0 + c))
                    if name[0] == "p":
                        for own in (32 * c, 64 + 32 * c):
                            other = 32 * (own // 32 ^ 1)
                            last = nc.vector.scalar_tensor_tensor(
                                d[other:other + 32, :], r1[own:own + 32, :], masks[own:own + 32, scale + c:scale + c + 1],
                                d[own:own + 32, :].bitcast(F32), ALU.mult, ALU.subtract)
                    elif scale is None:
                        last = nc.vector.tensor_tensor(d[1][:], r1[:], d[0][:].bitcast(F32), ALU.subtract)
                    else:
                        last = nc.vector.scalar_tensor_tensor(d[1][:], r1[:], masks[:, scale + c:scale + c + 1],
                                                              d[0][:].bitcast(F32), ALU.mult, ALU.subtract)
                    last.then_inc(s_rope_lo.sem, 1)

            def add_output(l, b, name):
                i = TILE[name]
                n = int(name[2])
                dve.wait_ge(s_mm.sem, s_mm.half_at(l, b, DV_MM + i))
                if name[1] == "b":
                    dve.wait_ge(s_xo.sem, s_xo.half_at(l, b, OUTS[f"oa{n}"]))
                else:
                    dve.wait_ge(s_x1, 2 * 16)
                    dve.wait_ge(s_xf.sem, s_xf.layer_at(l, -1))
                xn = x[:, bass.ds(b, 1), n, :].rearrange("p o t -> p (o t)")
                nc.vector.tensor_tensor(xn, xn, bank[i % 2][:], ALU.add).then_inc(s_xo.sem, 1)

            def plain_lo(l, b, name):
                src = bank[TILE[name] % 2][:]
                hi, lo = plain_target(name)
                dve.wait_ge(s_plain_hi.sem, s_plain_hi.half_at(l, b, PLAIN[name]))
                if name[:2] == "qn":
                    last = nc.vector.scalar_tensor_tensor(lo, src, MLA_SCALE, hi.bitcast(F32), ALU.mult, ALU.subtract)
                else:
                    last = nc.vector.tensor_tensor(lo, src, hi.bitcast(F32), ALU.subtract)
                last.then_inc(s_plain_lo.sem, 1)

            def stat_rsqrt(l, b, name, link):
                n = STATS.index(name)
                dve.wait_ge(s_rb.sem, s_rb.half_at(l, b, n - 1))
                width = {"ckv": KVL, "cq": QL, "n": D}.get(name, P)
                rsqrt_diagonal(link, width, bank[tail][:, 0:NT], (s_st.sem, s_st.half_at(l, b, n)), s_dg.sem)

            def stat_apply(l, b, name):
                dve.wait_ge(s_rb.sem, s_rb.half_at(l, b, STATS.index(name)))
                for q, n in enumerate(SQUARES[name]):
                    dst, src = normed_target(name, q)
                    if name[0] == "y":
                        dve.wait_ge(s_oc.sem, s_oc.half_at(l, b, int(name[1])))
                        nc.vector.tensor_tensor(src, src, bank[tail][:], ALU.mult).then_inc(s_t.sem, 1)
                    else:
                        dve.wait_ge(s_latent.sem, s_latent.half_at(l, b, LATENT["ckv" if name == "ckv" else f"cq{q}"]))
                        o = 3 if name == "ckv" else 1 + q
                        nc.vector.scalar_tensor_tensor(src, src, gsmall[:, bass.ds(l * 4 + o, 1)], bank[tail][:], ALU.mult,
                                                       ALU.mult).then_inc(s_t.sem, 1)

            def stat_lo(l, b, name):
                for q, n in enumerate(SQUARES[name]):
                    dst, src = normed_target(name, q)
                    dve.wait_ge(s_t_hi.sem, s_t_hi.half_at(l, b, n))
                    nc.vector.tensor_tensor(dst[1], src, dst[0].bitcast(F32), ALU.subtract).then_inc(s_t_lo.sem, 1)

            def combine(l, b, i, link):
                evs = [2 * i, 2 * i + 1] if i < 16 else [32 + i - 16]
                dve.wait_ge(s_exp.sem, s_exp.half_at(l, b, evs[-1]))
                if i < 16:
                    link(nc.vector.reciprocal(rc[:, 0:2], ls[:, evs[0]:evs[1] + 1]))
                    link(nc.vector.tensor_tensor(rc[:, 2:4], rc[:, 0:2], lamv[:, bass.ds(l * 2, 2)], ALU.mult))
                    p0, p1 = e[e_buffer(evs[0])][:], e[e_buffer(evs[1])][:]
                    link(nc.vector.tensor_scalar(p0, p0, rc[:, 2:3], None, ALU.mult))
                    nc.vector.scalar_tensor_tensor(p0, p1, rc[:, 3:4], p0, ALU.mult, ALU.add).then_inc(s_prob.sem, 1)
                else:
                    link(nc.vector.reciprocal(rc[:, 0:1], ls[:, evs[0]:evs[0] + 1]))
                    p0 = e[e_buffer(evs[0])][:]
                    nc.vector.tensor_scalar(p0, p0, rc[:, 0:1], None, ALU.mult).then_inc(s_prob.sem, 1)

            link, n = chain(lambda j: s_link.layer_at(0, j))
            norm_rsqrt("first", 0, 0, link)
            assert n[0] == RSQRT_LINKS, n
            dve.wait_ge(s_cs, 16)
            with dve.Fori(0, L) as l:
                norm_halves("first", l)
                with dve.Fori(0, B) as b:
                    link, n = chain(lambda j: s_link.half_at(l, b, j))
                    for step in VECTOR_ORDER:
                        kind, what = step[0], step[-1]
                        if kind == "V":
                            for m in range(NT):
                                dve.wait_ge(s_plain_hi.sem, s_plain_hi.half_at(l, b, m))
                                nc.vector.tensor_tensor(v[1][:, m, :], bank[2 + m][:], v[0][:, m, :].bitcast(F32),
                                                        ALU.subtract).then_inc(s_plain_lo.sem, 1)
                        elif kind == "RP":
                            rope(l, b, what)
                        elif kind == "RL":
                            rope_los(l, b, what)
                        elif kind == "XO":
                            add_output(l, b, what)
                        elif kind == "PL":
                            plain_lo(l, b, what)
                        elif kind == "MX":
                            for ev in ([2 * what, 2 * what + 1] if what < 16 else [16 + what]):
                                dve.wait_ge(s_score.sem, s_score.half_at(l, b, ev))
                                nc.vector.tensor_reduce(mx[:, ev:ev + 1], bank[2 + ev % 3][:], AX_X, ALU.max,
                                                        negate=True).then_inc(s_max.sem, 1)
                        elif kind == "CB":
                            combine(l, b, what, link)
                        elif kind == "TL":
                            dve.wait_ge(s_at_hi.sem, s_at_hi.half_at(l, b, what))
                            hi, lo = [aT[what // 2 % 2][s][:, :, (what % 2) * P:(what % 2 + 1) * P] for s in range(2)]
                            nc.vector.tensor_tensor(lo, bank[5][:].rearrange("p (k q) -> p k q", k=NT), hi.bitcast(F32),
                                                    ALU.subtract).then_inc(s_at_lo.sem, 1)
                        elif kind == "YL":
                            hi, lo = ymla[what - H]
                            dve.wait_ge(s_ym_hi.sem, s_ym_hi.half_at(l, b, what - H))
                            nc.vector.tensor_tensor(lo[:], bank[6][:], hi[:].bitcast(F32), ALU.subtract).then_inc(s_ym_lo.sem, 1)
                        elif kind == "RQ":
                            stat_rsqrt(l, b, what, link)
                        elif kind == "AP":
                            stat_apply(l, b, what)
                        elif kind == "AL":
                            stat_lo(l, b, what)
                        elif kind == "AN":
                            norm_apply("tail", l, b, what)
                        elif kind == "LN":
                            norm_lo("tail", l, b, what)
                    assert n[0] == LINKS_HALF, (n, LINKS_HALF)
                link, n = chain(lambda j: s_link.layer_at(l, RSQRT_LINKS + B * LINKS_HALF + j))
                for k in range(KT):
                    last_add(l, k)
                norm_rsqrt("last", l, 0, link)
                norm_halves("last", l)
                with dve.Fori(0, FC) as c:
                    for ev in range(4):
                        tt, b = ev // 2, ev % 2
                        dve.wait_ge(s_silu.sem, s_silu.step_at(l, c, ev))
                        dve.wait_ge(s_mm.sem, s_mm.step_at(l, c, 2 * ev + 1))
                        dve.wait_ge(s_u_lo.sem, s_u_lo.step_at(l, c, ev - 2))
                        nc.vector.tensor_tensor(gated[ev % 2][:], bank[2 + ev % 2][:], silu[ev % 2][:], ALU.mult).then_inc(s_gated.sem, 1)
                        dve.wait_ge(s_u_hi.sem, s_u_hi.step_at(l, c, ev))
                        nc.vector.tensor_tensor(u[tt][b][1][:], gated[ev % 2][:], u[tt][b][0][:].bitcast(F32),
                                                ALU.subtract).then_inc(s_u_lo.sem, 1)
                    for b in range(B):
                        for n in range(KT):
                            ev = b * KT + n
                            dve.wait_ge(s_mm.sem, s_mm.step_at(l, c, 8 + ev))
                            dve.wait_ge(s_xf.sem, s_xf.step_at(l, c, ev - 2 * KT))
                            nc.vector.tensor_tensor(x[:, b, n, :], x[:, b, n, :], bank[4 + ev % 4][:], ALU.add).then_inc(s_xf.sem, 1)
                link, n = chain(lambda j: s_link.layer_at(l, s_link.layer + j))
                norm_rsqrt("next", l, 0, link)
            n = [0]

            def final(ins):
                ins.then_inc(s_final, 1)
                n[0] += 1
                dve.wait_ge(s_final, n[0])

            def output(m):
                gain = g[:, 4 * L * KT + m % KT:4 * L * KT + m % KT + 1]
                nc.vector.scalar_tensor_tensor(y_out[:, m // KT, m % KT, :], x[:, m // KT, m % KT, :], gain,
                                               bank[tail if m < KT else 6][:], ALU.mult, ALU.mult).then_inc(s_final, 1)
                n[0] += 1
                assert n[0] == FINAL_T[m]

            for k in range(KT):
                dve.wait_ge(s_act, k + 1)
                if k == 0:
                    final(nc.vector.tensor_copy(acc_out[:], sq_out[:, 0, :]))
                else:
                    final(nc.vector.tensor_tensor(acc_out[:], acc_out[:], sq_out[:, k, :], ALU.add))
            assert n[0] == FINAL_ADD
            dve.wait_ge(s_rb.sem, s_rb.layer_at(L, 0))
            for m in range(4):
                output(m)
            rsqrt_diagonal(final, D, bank[6][:, 0:NT], (s_pe, 1), s_final, dg_out)
            n[0] += 1
            assert n[0] == FINAL_DG
            for m in range(4, B * KT):
                if m == KT:
                    dve.wait_ge(s_pe, 2)
                output(m)


def _tile(w, cols):
    a = w[:, cols]
    return a.reshape(-1, P, len(cols)).transpose(1, 0, 2).reshape(P, -1)


def _pair(base0, base1):
    half = np.arange(DH // 2)
    return np.concatenate([base0 + half, base1 + half, base0 + DH // 2 + half, base1 + DH // 2 + half])


def _attention_chunks(w_in, w_q_b, w_kv_b, w_o):
    width = H * 2 * DH
    parts = []
    for name in CHUNKS:
        if name[:2] == "dv":
            j = int(name[2])
            a = _tile(w_in[2 * j * P:2 * (j + 1) * P], np.arange(2 * width, 3 * width))
        elif name[0] in "qk" and name[1].isdigit():
            h = int(name[1])
            base = (width if name[0] == "k" else 0) + 2 * h * DH
            a = _tile(w_in, _pair(base, base + DH))
        elif name == "kpe":
            base = 3 * width + QL + KVL
            a = _tile(w_in, _pair(base, base))
        elif name == "ckv":
            a = _tile(w_in, 3 * width + QL + np.arange(KVL))
        elif name[:2] == "cq":
            a = _tile(w_in, 3 * width + int(name[2]) * P + np.arange(P))
        elif name == "pe":
            base = [h * (NOPE + ROPE) + NOPE for h in range(H)]
            a = _tile(w_q_b, np.concatenate([_pair(base[0], base[1]), _pair(base[2], base[3])]))
        elif name == "qn":
            a = _tile(w_q_b, np.concatenate([h * (NOPE + ROPE) + np.arange(NOPE) for h in range(H)]))
        elif name == "kvb":
            a = _tile(w_kv_b, np.concatenate([h * 2 * P + s * P + np.arange(P) for s in range(2) for h in range(H)]))
        else:
            rows = 0 if name[1] == "a" else H * P
            a = _tile(w_o[rows:rows + H * P], int(name[2]) * 2 * P + np.arange(2 * P))
        out = np.zeros((P, CH), w_in.dtype)
        out[:, :a.shape[1]] = a
        parts.append(out)
    return np.stack(parts)


def _ffn_chunks(w_gate, w_up, w_down):
    parts = []
    for c in range(FC):
        for f in (2 * c, 2 * c + 1):
            parts += [_tile(w_gate, f * P + np.arange(P)), _tile(w_up, f * P + np.arange(P))]
        for f in (2 * c, 2 * c + 1):
            parts.append(w_down[f * P:(f + 1) * P])
    return np.stack(parts)


def _tables():
    half = DH // 2
    inv = (1.0 / (np.float32(10000.0) ** (np.arange(half, dtype=np.float32) * np.float32(2.0) / np.float32(DH)))).astype(np.float32)
    ang = (np.arange(T, dtype=np.float32)[None, :] * inv[:, None]).astype(np.float32)
    cos = np.tile(np.cos(ang.astype(np.float64)), (4, 1))
    sin = np.tile(np.sin(ang.astype(np.float64)), (4, 1))
    sin[2 * half:] *= -1
    masks = np.zeros((P, 4))
    for c in range(2):
        rows = (np.arange(P) // half) % 2 == c
        masks[rows, c] = DIFF_SCALE
        masks[rows, 2 + c] = MLA_SCALE
    return np.concatenate([cos, sin, np.eye(P), masks], axis=1).astype(np.float32)


def kernel(x_prompt, x_sample, attn_norm, w_in, lam_q1, lam_k1, lam_q2, lam_k2, diff_subln, q_a_norm, w_q_b, kv_a_norm,
           w_kv_b, w_o, ffn_norm, w_gate, w_up, w_down, final_norm):
    import concourse.bacc as bacc
    from concourse.bass_utils import run_bass_kernel_spmd

    def features(a):
        return np.ascontiguousarray(a.T.reshape(-1, P, a.shape[0]).transpose(1, 0, 2))

    a = {k: np.asarray(val) for k, val in dict(
        x_prompt=x_prompt, x_sample=x_sample, attn_norm=attn_norm, w_in=w_in, lam_q1=lam_q1, lam_k1=lam_k1, lam_q2=lam_q2,
        lam_k2=lam_k2, diff_subln=diff_subln, q_a_norm=q_a_norm, w_q_b=w_q_b, kv_a_norm=kv_a_norm, w_kv_b=w_kv_b, w_o=w_o,
        ffn_norm=ffn_norm, w_gate=w_gate, w_up=w_up, w_down=w_down, final_norm=final_norm).items()}
    by_tile = lambda v: v.reshape(-1, P).T
    gains = [by_tile(a[n][l]) for l in range(L) for n in ("attn_norm", "attn_norm", "ffn_norm", "ffn_norm")]
    gains.append(by_tile(a["final_norm"]))
    for l in range(L):
        gains += [by_tile(a["diff_subln"][l]), by_tile(a["q_a_norm"][l]), by_tile(a["kv_a_norm"][l])]
    lam = [a[n][l] for pair in (("lam_q1", "lam_q2"), ("lam_k1", "lam_k2")) for l in range(L) for n in pair]
    arrays = {
        "xT": np.stack([features(a["x_prompt"][0]), features(a["x_sample"][0])]),
        "watt": np.concatenate([_attention_chunks(a["w_in"][l], a["w_q_b"][l], a["w_kv_b"][l], a["w_o"][l]) for l in range(L)]),
        "wffn": np.concatenate([_ffn_chunks(a["w_gate"][l], a["w_up"][l], a["w_down"][l]) for l in range(L)]),
        "tables": _tables(),
        "gains": np.ascontiguousarray(np.concatenate(gains, axis=1)),
        "lam": np.ascontiguousarray(np.broadcast_to(np.concatenate(lam)[None, :], (P, 8 * DH))),
    }
    nc = bacc.Bacc("TRN2", target_bir_lowering=False, num_devices=1)
    args = [nc.dram_tensor(f"in_{n}", v.shape, F32, kind="ExternalInput").ap() for n, v in arrays.items()]
    out = nc.dram_tensor("out_yT", (B, P, KT, T), F32, kind="ExternalOutput").ap()
    encoder_trunk(nc, *args, out)
    r = run_bass_kernel_spmd(nc, [{f"in_{n}": v for n, v in arrays.items()}], core_ids=[0])
    y = r.results[0]["out_yT"]
    return tuple(np.ascontiguousarray(y[b].transpose(2, 1, 0).reshape(1, T, D)) for b in range(B))
```
